# Optimizing a Trainium2 kernel written in Bass

```python
import jax
import jax.numpy as jnp
from jax import lax
import numpy as np

D_MODEL = 1024
BATCH = 1
SEQ = 256
DEPTH = 2

FOX_HEADS = 8
FOX_DIM = 64
DSA_HEADS = 8
DSA_DIM = 64
IDX_HEADS = 8
IDX_DIM = 32
DSA_MAX_TOPK = 256
RET_HEADS = 4
RET_QK_DIM = 64
RET_V_DIM = 128
RET_CHUNK = 128
Q_BLOCK = 128
FFN_HIDDEN = ((8 * D_MODEL + 3 * 256 - 1) // (3 * 256)) * 256
ROPE_THETA = 10000.0
NORM_EPS = 1e-6

FOX_W = FOX_HEADS * FOX_DIM
DSA_W = DSA_HEADS * DSA_DIM
RET_QK_W = RET_HEADS * RET_QK_DIM
RET_V_W = RET_HEADS * RET_V_DIM
N_BRANCH = 3
IN_SIZES = (FOX_W, FOX_W, FOX_W, FOX_HEADS,
            DSA_W, DSA_DIM, DSA_DIM, IDX_HEADS * IDX_DIM, IDX_DIM, IDX_HEADS,
            RET_QK_W, RET_QK_W, RET_V_W, RET_V_W,
            N_BRANCH * D_MODEL)
IN_COLS = sum(IN_SIZES)

kernel_name = 'hybrid_fox_dsa_retention_block'

def split_columns(z):
    points = []
    acc = 0
    for s in IN_SIZES[:-1]:
        acc += s
        points.append(acc)
    return jnp.split(z, points, axis=-1)

def rms_norm(x, g):
    xf = x.astype(jnp.float32)
    y = xf * lax.rsqrt(jnp.mean(xf * xf, axis=-1, keepdims=True) + NORM_EPS)
    return (y * g.astype(jnp.float32)).astype(x.dtype)

def apply_rope(x, pos):
    half = x.shape[-1] // 2
    inv_freq = ROPE_THETA ** (-jnp.arange(half, dtype=jnp.float32) / half)
    ang = pos.astype(jnp.float32)[:, None] * inv_freq[None, :]
    cos = jnp.cos(ang)[:, None, :]
    sin = jnp.sin(ang)[:, None, :]
    xf = x.astype(jnp.float32)
    x1, x2 = xf[..., :half], xf[..., half:]
    return jnp.concatenate([x1 * cos - x2 * sin, x2 * cos + x1 * sin], axis=-1).astype(x.dtype)

def fox_attention(q, k, v, log_f):
    b, l, h, d = q.shape
    nb = l // Q_BLOCK
    scale = d ** -0.5
    c = jnp.cumsum(log_f, axis=1).transpose(0, 2, 1)
    kpos = jnp.arange(l)
    qb = q.reshape(b, nb, Q_BLOCK, h, d).swapaxes(0, 1)
    cb = c.reshape(b, h, nb, Q_BLOCK).transpose(2, 0, 1, 3)

    def block(args):
        i, qi, ci = args
        qpos = i * Q_BLOCK + jnp.arange(Q_BLOCK)
        s = jnp.einsum('bqhd,bkhd->bhqk', qi, k).astype(jnp.float32) * scale
        s = s + ci[..., :, None] - c[:, :, None, :]
        s = jnp.where(kpos[None, :] <= qpos[:, None], s, -jnp.inf)
        p = jax.nn.softmax(s, axis=-1).astype(v.dtype)
        return jnp.einsum('bhqk,bkhd->bqhd', p, v)

    out = lax.map(block, (jnp.arange(nb), qb, cb))
    return out.swapaxes(0, 1).reshape(b, l, h, d)

def dsa_attention(q, k, v, iq, ik, iw):
    b, l, h, d = q.shape
    nb = l // Q_BLOCK
    topk = min(DSA_MAX_TOPK, l // 4)
    scale = d ** -0.5
    idx_scale = (IDX_DIM * IDX_HEADS) ** -0.5
    kpos = jnp.arange(l)
    qb = q.reshape(b, nb, Q_BLOCK, h, d).swapaxes(0, 1)
    iqb = iq.reshape(b, nb, Q_BLOCK, IDX_HEADS, IDX_DIM).swapaxes(0, 1)
    iwb = iw.reshape(b, nb, Q_BLOCK, IDX_HEADS).swapaxes(0, 1)
    gather = jax.vmap(lambda table, rows: table[rows])

    def block(args):
        i, qi, iqi, iwi = args
        qpos = i * Q_BLOCK + jnp.arange(Q_BLOCK)
        causal = kpos[None, :] <= qpos[:, None]
        rel = jax.nn.relu(jnp.einsum('bqhd,bkd->bqhk', iqi, ik).astype(jnp.float32))
        score = jnp.einsum('bqhk,bqh->bqk', rel, iwi.astype(jnp.float32)) * idx_scale
        score = jnp.where(causal[None], score, -jnp.inf)
        _, sel = lax.top_k(score, topk)
        valid = sel <= qpos[None, :, None]
        kg = gather(k, sel)
        vg = gather(v, sel)
        s = jnp.einsum('bqhd,bqkd->bqhk', qi, kg).astype(jnp.float32) * scale
        s = jnp.where(valid[:, :, None, :], s, -jnp.inf)
        p = jax.nn.softmax(s, axis=-1).astype(v.dtype)
        return jnp.einsum('bqhk,bqkd->bqhd', p, vg)

    out = lax.map(block, (jnp.arange(nb), qb, iqb, iwb))
    return out.swapaxes(0, 1).reshape(b, l, h, d)

def retention(q, k, v):
    b, l, h, dk = q.shape
    dv = v.shape[-1]
    n = l // RET_CHUNK
    log_g = jnp.log1p(-(2.0 ** (-5.0 - jnp.arange(h, dtype=jnp.float32))))
    pos = jnp.arange(RET_CHUNK, dtype=jnp.float32)
    diff = pos[:, None] - pos[None, :]
    decay_in = jnp.where(diff >= 0, jnp.exp(jnp.maximum(diff, 0.0)[None] * log_g[:, None, None]), 0.0)
    decay_q = jnp.exp((pos + 1.0)[None] * log_g[:, None])
    decay_k = jnp.exp((RET_CHUNK - 1.0 - pos)[None] * log_g[:, None])
    decay_chunk = jnp.exp(RET_CHUNK * log_g)

    def chunks(t):
        return t.astype(jnp.float32).reshape(b, n, RET_CHUNK, h, t.shape[-1]).transpose(1, 0, 3, 2, 4)

    qc = chunks(q) * (dk ** -0.5)
    kc = chunks(k)
    vc = chunks(v)

    def step(state, inp):
        qi, ki, vi = inp
        attn = jnp.einsum('bhid,bhjd->bhij', qi, ki) * decay_in
        inner = jnp.einsum('bhij,bhje->bhie', attn, vi)
        cross = jnp.einsum('bhid,bhde->bhie', qi, state) * decay_q[..., None]
        state = decay_chunk[:, None, None] * state + jnp.einsum('bhjd,bhje->bhde', ki * decay_k[..., None], vi)
        return state, inner + cross

    state0 = jnp.zeros((b, h, dk, dv), jnp.float32)
    _, out = lax.scan(step, state0, (qc, kc, vc))
    return out.transpose(1, 0, 3, 2, 4).reshape(b, l, h, dv).astype(v.dtype)

def hybrid_layer(x, ln1_g, w_in, fox_b_f, fox_q_norm, fox_k_norm, dsa_q_norm, dsa_k_norm,
                 ret_out_norm, w_fox_out, w_dsa_out, w_ret_out, w_o, ln2_g, w_ffn_in, w_ffn_out):
    b, l, _ = x.shape
    pos = jnp.arange(l)
    hdn = rms_norm(x, ln1_g)
    (fq, fk, fv, ff, dq, dk, dv, iq, ik, iw, rq, rk, rv, rg, zg) = split_columns(hdn @ w_in)

    fq = rms_norm(fq.reshape(b, l, FOX_HEADS, FOX_DIM), fox_q_norm)
    fk = rms_norm(fk.reshape(b, l, FOX_HEADS, FOX_DIM), fox_k_norm)
    fv = fv.reshape(b, l, FOX_HEADS, FOX_DIM)
    log_f = jax.nn.log_sigmoid(ff.astype(jnp.float32) + fox_b_f.astype(jnp.float32))
    y_a = fox_attention(fq, fk, fv, log_f).reshape(b, l, FOX_W)

    dq = apply_rope(rms_norm(dq.reshape(b, l, DSA_HEADS, DSA_DIM), dsa_q_norm), pos)
    dk = apply_rope(rms_norm(dk, dsa_k_norm)[:, :, None, :], pos)[:, :, 0, :]
    iq = apply_rope(iq.reshape(b, l, IDX_HEADS, IDX_DIM), pos)
    ik = apply_rope(ik[:, :, None, :], pos)[:, :, 0, :]
    y_b = dsa_attention(dq, dk, dv, iq, ik, iw).reshape(b, l, DSA_W)

    rq = apply_rope(rq.reshape(b, l, RET_HEADS, RET_QK_DIM), pos)
    rk = apply_rope(rk.reshape(b, l, RET_HEADS, RET_QK_DIM), pos)
    rv = rv.reshape(b, l, RET_HEADS, RET_V_DIM)
    y_c = rms_norm(retention(rq, rk, rv), ret_out_norm).reshape(b, l, RET_V_W) * jax.nn.silu(rg)

    gates = jax.nn.sigmoid(zg).reshape(b, l, N_BRANCH, D_MODEL)
    merged = (gates[:, :, 0] * (y_a @ w_fox_out)
              + gates[:, :, 1] * (y_b @ w_dsa_out)
              + gates[:, :, 2] * (y_c @ w_ret_out))
    x = x + merged @ w_o

    g, u = jnp.split(rms_norm(x, ln2_g) @ w_ffn_in, 2, axis=-1)
    return x + (jax.nn.silu(g) * u) @ w_ffn_out

def setup_inputs(seed: int = 0) -> dict:
    key = jax.random.key(seed)
    ks = jax.random.split(key, 17)

    def nrm(k, shape, scale):
        return jax.random.normal(k, shape, jnp.float32) * scale

    res_scale = (2.0 * DEPTH) ** -0.5
    return {
        'x': nrm(ks[0], (BATCH, SEQ, D_MODEL), 1.0),
        'ln1_g': 1.0 + nrm(ks[1], (DEPTH, D_MODEL), 0.05),
        'w_in': nrm(ks[2], (DEPTH, D_MODEL, IN_COLS), D_MODEL ** -0.5),
        'fox_b_f': 3.0 + nrm(ks[3], (DEPTH, FOX_HEADS), 0.5),
        'fox_q_norm': 1.0 + nrm(ks[4], (DEPTH, FOX_DIM), 0.05),
        'fox_k_norm': 1.0 + nrm(ks[5], (DEPTH, FOX_DIM), 0.05),
        'dsa_q_norm': 1.0 + nrm(ks[6], (DEPTH, DSA_DIM), 0.05),
        'dsa_k_norm': 1.0 + nrm(ks[7], (DEPTH, DSA_DIM), 0.05),
        'ret_out_norm': 1.0 + nrm(ks[8], (DEPTH, RET_HEADS, RET_V_DIM), 0.05),
        'w_fox_out': nrm(ks[9], (DEPTH, FOX_W, D_MODEL), FOX_W ** -0.5),
        'w_dsa_out': nrm(ks[10], (DEPTH, DSA_W, D_MODEL), DSA_W ** -0.5),
        'w_ret_out': nrm(ks[11], (DEPTH, RET_V_W, D_MODEL), RET_V_W ** -0.5),
        'w_o': nrm(ks[12], (DEPTH, D_MODEL, D_MODEL), D_MODEL ** -0.5 * res_scale),
        'ln2_g': 1.0 + nrm(ks[13], (DEPTH, D_MODEL), 0.05),
        'w_ffn_in': nrm(ks[14], (DEPTH, D_MODEL, 2 * FFN_HIDDEN), D_MODEL ** -0.5),
        'w_ffn_out': nrm(ks[15], (DEPTH, FFN_HIDDEN, D_MODEL), FFN_HIDDEN ** -0.5 * res_scale),
    }

def reference(x, ln1_g, w_in, fox_b_f, fox_q_norm, fox_k_norm, dsa_q_norm, dsa_k_norm,
              ret_out_norm, w_fox_out, w_dsa_out, w_ret_out, w_o, ln2_g, w_ffn_in, w_ffn_out):
    for i in range(DEPTH):
        x = hybrid_layer(x, ln1_g[i], w_in[i], fox_b_f[i], fox_q_norm[i], fox_k_norm[i],
                         dsa_q_norm[i], dsa_k_norm[i], ret_out_norm[i], w_fox_out[i],
                         w_dsa_out[i], w_ret_out[i], w_o[i], ln2_g[i], w_ffn_in[i], w_ffn_out[i])
    return x


_drawn_inputs = setup_inputs


def setup_inputs(seed=0):
    import zlib

    import numpy as np

    out = dict(_drawn_inputs(seed))
    spreads = {}
    factors = {'fox_q_norm': 8.0,
     'fox_k_norm': 8.0,
     'dsa_q_norm': 8.0,
     'dsa_k_norm': 8.0,
     'ret_out_norm': 4.727}
    for name, (base, spread) in spreads.items():
        noise = np.random.default_rng([zlib.crc32(name.encode()), seed]).standard_normal(out[name].shape)
        drawn = base * np.exp(spread * noise) if base else spread * noise
        out[name] = jnp.asarray(drawn.astype(out[name].dtype))
    for name, factor in factors.items():
        out[name] = (out[name] * factor).astype(out[name].dtype)
    return out
```

```python
import numpy as np
import concourse.bass as bass
from concourse import mybir
from contextlib import ExitStack

D, SEQ, DEPTH, P = 1024, 256, 2, 128
T = SEQ // P
H, HD, IH, ID, RH, RV = 8, 64, 8, 32, 4, 128
FF = 2816
TOPK = 64
EPS = 1e-6
FV, FF_, DQ, DV, IQ, IW = 1024, 1536, 1544, 2120, 2184, 2472
RQ, RVC, RG, ZG = 2480, 2992, 3504, 4016
MIX = ZG
IN_COLS = ZG + 3 * D
NEG, TAKEN, TAKEN_CUT = -1e30, -3e38, -2e38

COL = 512
RING = 4
MIX_TILES, GATE_TILES, FF_TILES = 8, 6, FF // 256
U_IN, U_BR, U_WO = 0, 56, 68
U_FI, U_FO, UNITS = 76, 120, 144
SLOT_UNITS = UNITS // RING


def rope_and_masks():
    f = np.float32
    pos = np.arange(SEQ, dtype=f)

    def rope(half):
        inv = (f(10000.0) ** (-np.arange(half, dtype=f) / f(half))).astype(f)
        ang = (pos[:, None] * inv[None]).astype(f).astype(np.float64)
        c, s = np.cos(ang).astype(f), np.sin(ang).astype(f)
        both = np.concatenate([c, c, -s, s], 1)
        return both.reshape(T, P, 2, 2 * half).transpose(1, 2, 0, 3).reshape(P, -1)

    i = np.arange(P)
    causal = np.where(i[None] <= i[:, None], 0.0, NEG)
    mask = np.concatenate([np.zeros((P, P)), causal], 1)
    upto = (i[:, None] <= i[None]).astype(f)
    log_g = np.log1p(-(2.0 ** (-5.0 - np.arange(RH))))
    diff = np.arange(2 * P)[None] - i[:, None]
    dec = [np.where(diff >= 0, np.exp(np.maximum(diff, 0) * g), 0) * RETQK_SCALE for g in log_g]
    decay = np.concatenate([np.concatenate([d, d[:, :P]], 1) for d in dec], 1)
    return [np.ascontiguousarray(a.astype(f)) for a in (
        np.concatenate([np.eye(P), upto, np.ones((P, P)), mask], 1),
        np.concatenate([rope(HD // 2), rope(ID // 2), decay], 1))]


RETQK_SCALE = 64 ** -0.5
C_ID, C_UPTO, C_ONES, C_MASK, C1_COLS = 0, 128, 256, 384, 640
R_COS64, R_SIN64, R_COS32, R_SIN32, R_DECAY = 0, 128, 256, 320, 384
C2_COLS = R_DECAY + RH * 3 * P
G_FQ, G_FK, G_DQ, G_DK, G_RET, G_B, G_COLS = 0, 64, 128, 192, 256, 768, 776
TQ_IDX, TQ_DSA, TQ_RET, TQ_COLS = 0, 384, 1024, 1536
T_BLOCKS = [(0, 1), (2,), (3, 4), (5, 6), (7,), (8, 9), (10, 11)]
B_IK, B_DQ, B_DK, B_RQ, B_RK = 2, 3, 7, 8, 10

S_N1, S_YT, S_MG, S_N2, S_HID, SPLITS = 0, 4, 10, 14, 18, 29


def small_bank_plan():
    order = [("n1", j, j) for j in range(4)]
    order += [("t", 0, 0), ("t", 1, 1), ("cum", 0, 2)]
    order += [("idx", h, h % 2) for h in range(IH)]
    order += [("t", 2, 2), ("t", 3, 3), ("t", 4, 0), ("t", 5, 1), ("t", 6, 2)]
    for kind in "fd":
        for h in range(H):
            if kind == "f" and h % 2 == 0:
                order += [("fq", h // 2, 0), ("fk", h // 2, 1)]
            order += [(kind + "s", h, h % 2), (kind + "p", h, 2)]
            if h % 4 == 0:
                order.append((kind + "o", h // 4, 3))
    for h in range(RH):
        order.append(("rs", h, h % 2))
        if h % 2 == 0:
            order.append(("ro", h // 2, 3))
    order += [("yt", j, j % 4) for j in range(6)]
    order += [("mg", j, j) for j in range(4)]
    order += [("n2", j, j) for j in range(4)]
    order += [("hid", n, 2 + n % 2) for n in range(FF_TILES)]
    uses, plan = [0] * 4, {}
    for name, j, bank in order:
        plan[name, j] = (bank, uses[bank])
        uses[bank] += 1
    return plan, uses


PLAN, BANK_USES = small_bank_plan()


def last_unit(tile):
    if tile < 14:
        return 4 * tile + 3
    if tile < 20:
        return U_BR + 2 * (tile - 14) + 1
    if tile < 22:
        return U_WO + 4 * (tile - 20) + 3
    if tile < 33:
        return U_FI + 4 * (tile - 22) + 3
    return U_FO + 12 * (tile - 33) + 11


DVE_LINKS, POOL_LINKS = 50, 8


def build(nc, x, w_in, w_fox_out, w_dsa_out, w_ret_out, w_o, w_ffn_in, w_ffn_out,
          ln1_g, ln2_g, fox_b_f, fox_q_norm, fox_k_norm, dsa_q_norm, dsa_k_norm, ret_out_norm,
          table1, table2, out):
    f32, f32r = mybir.dt.float32, mybir.dt.float32r
    ALU, ACT, AX = mybir.AluOpType, mybir.ActivationFunctionType, mybir.AxisListType
    ds = bass.ds
    with ExitStack() as ctx:
        def sb(name, shape, dt=f32):
            return ctx.enter_context(nc.sbuf_tensor(name, shape, dt))

        def sem(name):
            return ctx.enter_context(nc.semaphore(name))

        x_sb = sb("x_sb", [P, T, D])
        nrm = sb("nrm", [P, T, D])
        act_hi = sb("act_hi", [P, 8, SEQ], f32r)
        act_lo = sb("act_lo", [P, 8, SEQ], f32r)
        raw = sb("raw", [P, RING, 2, COL])
        w_hi = sb("w_hi", [P, RING, 2, COL], f32r)
        w_lo = sb("w_lo", [P, RING, 2, COL], f32r)
        con = sb("con", [P, C1_COLS])
        rope = sb("rope", [P, C2_COLS])
        gains = sb("gains", [P, DEPTH, G_COLS])
        gain = sb("gain", [P, G_COLS])
        lnrows = sb("lnrows", [2 * DEPTH * 8, P])
        lncols = sb("lncols", [P, 2 * DEPTH * 8])
        lncol = sb("lncol", [P, 2, 8])
        gates = sb("gates", [P, T, 3 * D])
        tq = sb("tq", [P, T, TQ_COLS])
        y = tq
        qa = sb("qa", [P, T, 2 * H, HD + 2])
        iw = sb("iw", [P, T, IH])
        ssq = sb("ssq", [P, T, 25])
        xssq = sb("xssq", [P, T])
        xrstd = sb("xrstd", [P, T])
        half = sb("half", [P, T * 25])
        fbias = sb("fbias", [P, 4, T, H])
        lf = sb("lf", [P, T, H])
        nmax = sb("nmax", [P, 2, H, T])
        rsum = sb("rsum", [P, 2, T, H])
        rinv = sb("rinv", [P, 2, T, H])
        rssq = sb("rssq", [P, T, RH])
        top8 = sb("top8", [P, 2, 8])
        score = sb("score", [P, 3 * P])
        work = sb("work", [P, 3, 2, 3 * P])
        rel, prob, probT = (work[:, n] for n in range(3))
        hid = work[:, :, :, :].rearrange("p a b c -> p (a b c)")[:, 0:2 * T * 256] \
            .rearrange("p (b t c) -> p b t c", b=2, t=T)
        arena_at = (nc.sbuf_base + 31) // 32 * 32
        arena_words = T * MIX + 12 * SEQ + 8 * SEQ
        sb("arena", [P, arena_words])

        def at(name, shape, word, dt=f32):
            return nc.alloc_sbuf_tensor_at(name, shape, dt, offset=arena_at + 4 * word)

        z = at("z", [P, T, MIX], 0)
        tT = at("tT", [P, 12, SEQ], T * MIX)
        fT = at("fT", [HD + 2, 2, 2, 2, SEQ], T * MIX + 12 * SEQ)
        hT_hi = at("hT_hi", [P, FF // P, SEQ], 0, f32r)
        hT_lo = at("hT_lo", [P, FF // P, SEQ], FF // P * SEQ, f32r)
        pool_tmp = gates[:, :, 2 * D:2 * D + 2 * RH * HD].rearrange("p t (h d) -> p t h d", h=2 * RH)
        sig_rg = qa[:, :, :, :].rearrange("p t h d -> p (t h d)")[:, 0:T * COL].rearrange("p (t c) -> p t c", t=T)
        gated = qa[:, :, :, :].rearrange("p t h d -> p (t h d)")[:, T * COL:2 * T * COL].rearrange("p (t c) -> p t c", t=T)
        scr = nrm[:, :, :].rearrange("p t c -> p (t c)")

        acc = ctx.enter_context(nc.psum_tensor("acc", [P, 4, COL], f32))
        small = ctx.enter_context(nc.psum_tensor("small", [P, 4, COL], f32))

        consts_in = sem("consts_in")
        gain_in = sem("gain_in")
        resid = sem("resid")
        loaded = [sem(f"loaded{s}") for s in range(RING)]
        rounded = sem("rounded")
        split = sem("split")
        used = sem("used")
        z_ready = sem("z_ready")
        branch_taken = sem("branch_taken")
        small_full = [sem(f"small_full{b}") for b in range(4)]
        tr_hi, tr_split = sem("tr_hi"), sem("tr_split")
        x_squared, x_rstd, x_normed = sem("x_squared"), sem("x_rstd"), sem("x_normed")
        heads_squared, heads_ssq, heads_rstd = sem("heads_squared"), sem("heads_ssq"), sem("heads_rstd")
        f_abs, f_ln, f_lf, qa_ready = sem("f_abs"), sem("f_ln"), sem("f_lf"), sem("qa_ready")
        roped, ret_roped, t_ready = sem("roped"), sem("ret_roped"), sem("t_ready")
        fq_ready, fk_ready = sem("fq_ready"), sem("fk_ready")
        rel_ready, scored = sem("rel_ready"), sem("scored")
        s_ready, p_ready, pT_ready = sem("s_ready"), sem("p_ready"), sem("pT_ready")
        at_ready, ret_out, ret_rstd = sem("at_ready"), sem("ret_out"), sem("ret_rstd")
        sig_rg_ready, ret_gate, gates_ready = sem("sig_rg_ready"), sem("ret_gate"), sem("gates_ready")
        y_ready, merged, silu_ready, hid_ready = sem("y_ready"), sem("merged"), sem("silu_ready"), sem("hid_ready")
        param_ready = sem("param_ready")
        dve_order, act_order, pool_order = sem("dve_order"), sem("act_order"), sem("pool_order")
        ln_tp, ln_cols = sem("ln_tp"), sem("ln_cols")
        stored = sem("stored")
        carried = sem("carried")

        def full_at(layer, name, j):
            bank, k = PLAN[name, j]
            return small_full[bank], layer * BANK_USES[bank] + k + 1

        def released(layer, name, j):
            done, per_layer, n = {
                "n1": (tr_split, SPLITS, S_N1 + j), "yt": (tr_split, SPLITS, S_YT + j),
                "mg": (tr_split, SPLITS, S_MG + j), "n2": (tr_split, SPLITS, S_N2 + j),
                "t": (t_ready, 7, j), "cum": (qa_ready, 1, 0), "idx": (rel_ready, IH, j),
                "fq": (fq_ready, 4, j), "fk": (fk_ready, 4, j),
                "fs": (s_ready, 2 * H, j), "ds": (s_ready, 2 * H, H + j),
                "fp": (pT_ready, 2 * H, j), "dp": (pT_ready, 2 * H, H + j),
                "fo": (y_ready, 5, j), "do": (y_ready, 5, 2 + j),
                "rs": (at_ready, RH, j), "ro": (ret_out, 2, j)}[name]
            return done, layer * per_layer + n + 1

        def bank_free(layer, name, j):
            b, k = PLAN[name, j]
            before = next(step for step, place in PLAN.items() if place == (b, k - 1))
            return released(layer, *before)

        def own_wait(eng):
            eng.sem_inc(carried, 1)

        def tile_done(layer, tile, more=0):
            return used, layer * UNITS + more + RING + last_unit(tile) + 1

        def bank(name, j):
            return small[:, PLAN[name, j][0], :]

        block = ctx.enter_context(nc.Block())

        @block.sync
        def _(sp):
            sp.dma_start(con[:], table1).then_inc(consts_in, 16)
            sp.dma_start(x_sb[:], x.rearrange("b (t p) d -> p (b t) d", p=P)).then_inc(resid, 16)
            for n, g in enumerate((ln1_g, ln2_g)):
                sp.dma_start(lnrows[n * 8 * DEPTH:(n + 1) * 8 * DEPTH, :],
                             g.rearrange("l (k p) -> (l k) p", p=P)).then_inc(consts_in, 16)
            sp.dma_start(rope[:], table2).then_inc(consts_in, 16)

            def unit(layer, u, slot, dst, src):
                sp.wait_ge(split, layer * UNITS + u + 1)
                sp.dma_start(dst, src).then_inc(loaded[slot], 16)

            def rows(w, layer, r, col, cols, k=2):
                return w[ds(layer, 1), r * P:(r + k) * P, col:col + cols] \
                    .rearrange("a (k p) n -> p (a k) n", p=P)

            def rows_at(w, layer, r, col, k=2):
                return w[ds(layer, 1), r * P:(r + k) * P, ds(col, COL)] \
                    .rearrange("a (k p) n -> p (a k) n", p=P)

            with sp.Fori(0, DEPTH) as layer:
                for u in range(4):
                    unit(layer, u, u, raw[:, u], rows(w_in, layer, 2 * u, 0, COL))
                with sp.Fori(0, 3) as i:
                    for n in (1, 2):
                        for u in range(4):
                            unit(layer, i * 8 + n * 4 + u, u, raw[:, u],
                                 rows_at(w_in, layer, 2 * u, i * (2 * COL) + n * COL))
                for u in range(4):
                    unit(layer, 28 + u, u, raw[:, u, :, 0:MIX - 7 * COL],
                         rows(w_in, layer, 2 * u, 7 * COL, MIX - 7 * COL))
                for n in range(GATE_TILES):
                    for u in range(4):
                        unit(layer, 32 + 4 * n + u, u, raw[:, u], rows(w_in, layer, 2 * u, ZG + n * COL, COL))
                for ct in range(2):
                    for b, w in enumerate((w_fox_out, w_dsa_out, w_ret_out)):
                        for u in range(2):
                            n = U_BR + 6 * ct + 2 * b + u
                            unit(layer, n, n % RING, raw[:, n % RING], rows(w, layer, 2 * u, ct * COL, COL))
                for ct in range(2):
                    for u in range(4):
                        unit(layer, U_WO + 4 * ct + u, u, raw[:, u], rows(w_o, layer, 2 * u, ct * COL, COL))

                def ff_unit(n, u, s):
                    for k in range(2):
                        src = w_ffn_in[ds(layer, 1), (2 * u + k) * P:(2 * u + k + 1) * P, :] \
                            .rearrange("a p (g n) -> p (a g) n", g=2)[:, :, s]
                        sp.dma_start(raw[:, u, k].rearrange("p (g n) -> p g n", g=2), src) \
                            .then_inc(loaded[u], 16)
                for u in range(4):
                    sp.wait_ge(split, layer * UNITS + U_FI + u + 1)
                    ff_unit(0, u, slice(0, 256))
                with sp.Fori(0, 5) as i:
                    for n in (1, 2):
                        for u in range(4):
                            sp.wait_ge(split, layer * UNITS + i * 8 + (U_FI + n * 4 + u + 1))
                            ff_unit(n, u, ds(i * 512 + n * 256, 256))
                for ct in range(2):
                    for u in range(12):
                        k = 2 if u < 10 else 1
                        r = 2 * u if u < 11 else 21
                        n = U_FO + 12 * ct + u
                        unit(layer, n, n % RING, raw[:, n % RING, 0:k], rows(w_ffn_out, layer, r, ct * COL, COL, k))
            for t in range(T):
                sp.wait_ge(resid, 16 + 8 * DEPTH)
                sp.dma_start(out[0, t * P:(t + 1) * P, :], x_sb[:, t, :]).then_inc(stored, 16)
            sp.wait_ge(stored, 32)

        def loads_before(u):
            return u // RING + 1 + max(0, min(u, U_FO - 1) - U_FI + RING) // RING * (u >= U_FI)

        SLOT_LOADS = loads_before(UNITS - 1)
        assert SLOT_LOADS == SLOT_UNITS + FF_TILES

        @block.gpsimd
        def _(pool):
            links = [0]

            def link(ins, layer):
                links[0] += 1
                ins.then_inc(pool_order, 1)
                pool.wait_ge(pool_order, layer * POOL_LINKS + links[0] + 1)

            nc.gpsimd.memset(half[:], -0.5).then_inc(pool_order, 1)
            pool.wait_ge(pool_order, 1)
            pool.wait_ge(consts_in, 64)

            def rsqrt(layer, v, n, count, done, scale_q=False):
                own_wait(pool)
                link(nc.gpsimd.tensor_scalar(v, v, 1.0 / count, EPS, ALU.mult, ALU.add), layer)
                op = nc.gpsimd.tensor_tensor(v, v, half[:, 0:n], ALU.pow)
                if scale_q:
                    link(op, layer)
                    own_wait(pool)
                    nc.gpsimd.tensor_scalar(ssq[:, :, 0:H], ssq[:, :, 0:H], HD ** -0.5, None, ALU.mult)
                    op = nc.gpsimd.tensor_scalar(ssq[:, :, 2 * H:3 * H], ssq[:, :, 2 * H:3 * H],
                                                 HD ** -0.5, None, ALU.mult)
                op.then_inc(done, 1)

            with pool.Fori(0, DEPTH) as layer:
                pool.wait_ge(x_squared, 2 * layer + 1)
                rsqrt(layer, xssq[:], T, D, x_rstd)
                pool.wait_ge(heads_ssq, layer + 1)
                rsqrt(layer, ssq[:].rearrange("p t h -> p (t h)"), T * 25, HD, heads_rstd, True)
                rh = 2 * RH
                zr = z[:, :, RQ:RQ + rh * HD].rearrange("p t (h d) -> p t h d", h=rh)
                tr = tq[:, :, TQ_RET:TQ_COLS].rearrange("p t (h d) -> p t h d", h=rh)
                cos = rope[:, R_COS64:R_SIN64].rearrange("p (t d) -> p t d", t=T)
                sin = rope[:, R_SIN64:R_COS32].rearrange("p (t d) -> p t d", t=T)
                for t in range(T):
                    nc.gpsimd.tensor_tensor(tr[:, t], zr[:, t], cos[:, t].unsqueeze(1).broadcast_to([P, rh, HD]), ALU.mult)
                    for a in range(2):
                        b = 1 - a
                        last = nc.gpsimd.tensor_tensor(
                            pool_tmp[:, t, :, 32 * a:32 * a + 32], zr[:, t, :, 32 * b:32 * b + 32],
                            sin[:, t, 32 * a:32 * a + 32].unsqueeze(1).broadcast_to([P, rh, 32]), ALU.mult)
                    link(last, layer)
                    last = nc.gpsimd.tensor_tensor(tr[:, t], tr[:, t], pool_tmp[:, t], ALU.add)
                last.then_inc(ret_roped, 1)
                pool.wait_ge(sig_rg_ready, layer + 1)
                link(nc.gpsimd.tensor_tensor(sig_rg, sig_rg, z[:, :, RG:RG + COL], ALU.mult), layer)
                nc.gpsimd.tensor_tensor(sig_rg, sig_rg, gain[:, G_RET:G_RET + COL].unsqueeze(1)
                                        .broadcast_to([P, T, COL]), ALU.mult).then_inc(ret_gate, 1)
                pool.wait_ge(ret_out, 2 * layer + 2)
                rsqrt(layer, rssq[:].rearrange("p t h -> p (t h)"), T * RH, RV, ret_rstd)
                pool.wait_ge(x_squared, 2 * layer + 2)
                rsqrt(layer, xssq[:], T, D, x_rstd)
                assert links[0] == POOL_LINKS, links

        @block.scalar
        def _(act):
            act.sem_inc(z_ready, 1)
            act.wait_ge(ln_tp, 1)
            nc.scalar.activation(lncols[:], small[:, 0, 0:32], ACT.Copy).then_inc(ln_cols, 1)

            def round_unit(layer, u, slot, cols=COL, k=2, at=None):
                more, loads = at if at else (0, 0)
                act.wait_ge(loaded[slot], layer * (16 * SLOT_LOADS) + loads + 16 * loads_before(u))
                act.wait_ge(used, layer * UNITS + more + u + 1)
                nc.scalar.activation(w_hi[:, slot, 0:k, 0:cols], raw[:, slot, 0:k, 0:cols],
                                     ACT.Copy).then_inc(rounded, 1)

            def round_transposed(layer, name, j, step, dst, scale=None):
                act.wait_ge(*full_at(layer, name, j))
                src = bank(name, j).rearrange("p (k s) -> p k s", k=2)
                if scale is None:
                    nc.scalar.activation(dst, src, ACT.Copy).then_inc(tr_hi, 1)
                else:
                    for k in range(2):
                        last = nc.scalar.activation(dst[:, k], src[:, k], ACT.Copy, scale=scale[:, k:k + 1])
                    last.then_inc(tr_hi, 1)

            def square_x(layer, n):
                act.wait_ge(resid, layer * 8 + 16 + 4 * n)
                for t in range(T):
                    last = nc.scalar.activation(nrm[:, t], x_sb[:, t], ACT.Square, accum_out=xssq[:, t:t + 1])
                last.then_inc(x_squared, 1)

            def norm_hi(layer, name, n):
                for j in range(4):
                    round_transposed(layer, name, j, 0, act_hi[:, 2 * j:2 * j + 2], lncol[:, n, 2 * j:2 * j + 2])

            def evac(layer, tile, dst, cols=COL):
                act.wait_ge(*tile_done(layer, tile))
                for t in range(T):
                    last = nc.scalar.activation(dst[:, t], acc[:, 2 * (tile % 2) + t, 0:cols], ACT.Copy)
                last.then_inc(z_ready, 1)

            def attend(layer, kind, h):
                k = "fd".index(kind)
                act.wait_ge(s_ready, layer * 2 * H + k * H + h + 1)
                for t in range(T):
                    c = slice(0, P) if t == 0 else slice(P, 3 * P)
                    last = nc.scalar.activation(prob[:, h % 2, c], prob[:, h % 2, c], ACT.Exp,
                                                bias=nmax[:, k, h, t:t + 1], scale=-1.0,
                                                accum_out=rsum[:, k, t, h:h + 1])
                last.then_inc(p_ready, 1)

            def attend_T(layer, kind, h):
                act.wait_ge(*full_at(layer, kind + "p", h))
                nc.scalar.activation(probT[:, h % 2], bank(kind + "p", h)[:, 0:3 * P], ACT.Copy).then_inc(pT_ready, 1)

            with act.Fori(0, DEPTH) as layer:
                square_x(layer, 0)
                for c, g in ((G_FQ, fox_q_norm), (G_FK, fox_k_norm), (G_DQ, dsa_q_norm), (G_DK, dsa_k_norm),
                             (G_RET, ret_out_norm.rearrange("l h d -> l (h d)")), (G_B, fox_b_f)):
                    n = g.shape[-1]
                    act.dma_start(gain[:, c:c + n], g[ds(layer, 1), :].broadcast_to([P, n])).then_inc(gain_in, 16)
                for u in range(3):
                    round_unit(layer, u, u)
                act.wait_ge(param_ready, layer + 1)
                norm_hi(layer, "n1", 0)
                round_unit(layer, 3, 3)
                with act.Fori(0, 3) as i:
                    for n in (1, 2):
                        for u in range(4):
                            round_unit(layer, 4 * n + u, u, at=(i * 8, i * 32))
                            if u == 1:
                                act.wait_ge(*tile_done(layer, n - 1, i * 8))
                                for t in range(T):
                                    last = nc.scalar.activation(z[:, t, ds(i * (2 * COL) + (n - 1) * COL, COL)],
                                                                acc[:, 2 * (1 - n % 2) + t], ACT.Copy)
                                last.then_inc(z_ready, 1)
                for u in range(4):
                    round_unit(layer, 28 + u, u, MIX - 7 * COL)
                    if u == 1:
                        evac(layer, 6, z[:, :, 6 * COL:7 * COL])
                gate_units = iter(range(32, 56))

                def gate(count=1):
                    for _ in range(count):
                        u = next(gate_units)
                        round_unit(layer, u, u % RING)
                        n = u // 4
                        if u % 4 == 1:
                            if n == 8:
                                evac(layer, 7, z[:, :, 7 * COL:MIX], MIX - 7 * COL)
                            else:
                                if n == 12:
                                    act.wait_ge(ret_roped, layer + 1)
                                evac(layer, n - 1, gates[:, :, (n - 9) * COL:(n - 8) * COL])

                gate(2)
                act.wait_ge(z_ready, layer * 14 + 9)
                for t in range(T):
                    nc.scalar.activation(qa[:, t, :, 0:HD], z[:, t, 0:2 * H * HD]
                                         .rearrange("p (h d) -> p h d", d=HD), ACT.Square)
                nc.scalar.activation(tq[:, :, TQ_DSA:TQ_DSA + 9 * HD], z[:, :, DQ:DQ + 9 * HD],
                                     ACT.Square).then_inc(heads_squared, 1)
                gate(2)
                nc.scalar.preload_act_table_set("natural_log_exp_and_others")
                act.wait_ge(f_abs, layer + 1)
                nc.scalar.activation(fbias[:, 2], fbias[:, 1], ACT.Exp).then_inc(act_order, 1)
                act.wait_ge(act_order, layer + 1)
                nc.scalar.activation(fbias[:, 3], fbias[:, 2], ACT.Ln, bias=1.0).then_inc(f_ln, 1)

                def t_evac(j):
                    act.wait_ge(*full_at(layer, "t", j))
                    b = T_BLOCKS[j]
                    nc.scalar.activation(tT[:, b[0]:b[-1] + 1], bank("t", j)[:, 0:len(b) * SEQ]
                                         .rearrange("p (b s) -> p b s", s=SEQ), ACT.Copy).then_inc(t_ready, 1)

                def index(h):
                    act.wait_ge(*full_at(layer, "idx", h))
                    act.wait_ge(scored, layer * 2 * IH + 2 * h - 2) if h >= 2 else None
                    nc.scalar.activation(rel[:, h % 2], bank("idx", h)[:, 0:3 * P], ACT.Relu)\
                        .then_inc(rel_ready, 1)

                t_evac(0)
                t_evac(1)
                gate(4)
                for h in range(IH):
                    index(h)
                    if h % 2:
                        gate(1)
                for j in range(2, 7):
                    t_evac(j)
                gate(2)

                def fox_q(hp):
                    act.wait_ge(*full_at(layer, "fq", hp))
                    nc.scalar.activation(fT[:, hp % 2, 0], bank("fq", hp)[0:HD + 2, :]
                                         .rearrange("p (h s) -> p h s", h=2), ACT.Copy).then_inc(fq_ready, 1)

                fox_q(0)
                for h in range(H):
                    gate(1)
                    if h % 2 and h < H - 1:
                        fox_q((h + 1) // 2)
                    attend(layer, "f", h)
                    attend_T(layer, "f", h)
                for h in range(H):
                    if h < 2:
                        gate(1)
                    attend(layer, "d", h)
                    attend_T(layer, "d", h)
                assert next(gate_units, None) is None
                evac(layer, 13, gates[:, :, 5 * COL:6 * COL])
                act.wait_ge(y_ready, layer * 5 + 4)
                nc.scalar.activation(sig_rg, z[:, :, RG:RG + COL], ACT.Sigmoid).then_inc(sig_rg_ready, 1)
                act.wait_ge(z_ready, layer * 14 + 15)
                nc.scalar.activation(gates[:], gates[:], ACT.Sigmoid).then_inc(gates_ready, 1)
                for r in range(2):
                    act.wait_ge(*full_at(layer, "ro", r))
                    src = bank("ro", r).rearrange("p (t h d) -> p t h d", t=T, h=2)
                    nc.scalar.activation(y[:, :, D + r * 2 * RV:D + (r + 1) * 2 * RV],
                                         bank("ro", r).rearrange("p (t c) -> p t c", t=T), ACT.Copy)
                    for t in range(T):
                        for h in range(2):
                            last = nc.scalar.activation(gated[:, t, (2 * r + h) * RV:(2 * r + h + 1) * RV], src[:, t, h], ACT.Square,
                                                        accum_out=rssq[:, t, 2 * r + h:2 * r + h + 1])
                    last.then_inc(ret_out, 1)
                for j in range(6):
                    round_transposed(layer, "yt", j, 0, hT_hi[:, 2 * j:2 * j + 2])
                for u in range(U_BR, U_WO):
                    round_unit(layer, u, u % RING)
                for u in range(2):
                    round_unit(layer, U_WO + u, u)
                for j in range(4):
                    round_transposed(layer, "mg", j, 0, act_hi[:, 2 * j:2 * j + 2])
                for u in range(2, 8):
                    round_unit(layer, U_WO + u, u % RING)
                square_x(layer, 1)
                for u in range(3):
                    round_unit(layer, U_FI + u, u)
                norm_hi(layer, "n2", 1)
                round_unit(layer, U_FI + 3, 3)

                def silu(n, b, more=0):
                    act.wait_ge(*tile_done(layer, 22 + n, more))
                    for t in range(T):
                        last = nc.scalar.activation(hid[:, b, t], acc[:, 2 * b + t, 0:256], ACT.Silu)
                    last.then_inc(silu_ready, 1)

                with act.Fori(0, 5) as i:
                    for n in (1, 2):
                        for u in range(4):
                            round_unit(layer, U_FI + 4 * n + u, u, at=(i * 8, i * 64))
                            if u == 1:
                                silu(n - 1, 1 - n % 2, i * 8)
                        b, k = PLAN["hid", n - 1]
                        act.wait_ge(small_full[b], layer * BANK_USES[b] + i + k + 1)
                        nc.scalar.activation(hT_hi[:, ds(i * 4 + 2 * (n - 1), 2)], small[:, b]
                                             .rearrange("p (k s) -> p k s", k=2), ACT.Copy).then_inc(tr_hi, 1)
                silu(10, 0)
                for u in range(3):
                    round_unit(layer, U_FO + u, u)
                round_transposed(layer, "hid", 10, 0, hT_hi[:, 20:22])
                for u in range(3, 24):
                    round_unit(layer, U_FO + u, u % RING, k=2 if u % 12 < 10 else 1)

        @block.vector
        def _(dve):
            links = [0]
            dve.sem_inc(split, RING)
            dve.sem_inc(hid_ready, 1)
            dve.wait_ge(consts_in, 64)
            dve.wait_ge(ln_cols, 1)

            with dve.Fori(0, DEPTH) as layer:
                def link(ins):
                    links[0] += 1
                    ins.then_inc(dve_order, 1)
                    return links[0]

                def after(n):
                    dve.wait_ge(dve_order, layer * DVE_LINKS + n)

                def split_unit(u, slot, cols=COL, k=2, more=0):
                    dve.wait_ge(rounded, layer * UNITS + more + u + 1)
                    nc.vector.tensor_tensor(w_lo[:, slot, 0:k, 0:cols], raw[:, slot, 0:k, 0:cols],
                                            w_hi[:, slot, 0:k, 0:cols].bitcast(f32), ALU.subtract).then_inc(split, 1)

                def split_transposed(name, j, step, hi, lo, scale=None):
                    dve.wait_ge(tr_hi, layer * SPLITS + step + 1)
                    src = bank(name, j).rearrange("p (k s) -> p k s", k=2)
                    if scale is None:
                        last = nc.vector.tensor_tensor(lo, src, hi.bitcast(f32), ALU.subtract)
                    else:
                        for k in range(2):
                            last = nc.vector.scalar_tensor_tensor(lo[:, k], src[:, k], scale[:, k:k + 1],
                                                                  hi[:, k].bitcast(f32), ALU.mult, ALU.subtract)
                    last.then_inc(tr_split, 1)

                def norm(n):
                    dve.wait_ge(x_rstd, 2 * layer + n + 1)
                    for t in range(T):
                        last = nc.vector.tensor_scalar(nrm[:, t], x_sb[:, t], xssq[:, t:t + 1], None, ALU.mult)
                    last.then_inc(x_normed, 1)

                def norm_lo(name, step, n):
                    for j in range(4):
                        split_transposed(name, j, step + j, act_hi[:, 2 * j:2 * j + 2], act_lo[:, 2 * j:2 * j + 2],
                                         lncol[:, n, 2 * j:2 * j + 2])

                for n in range(2):
                    last = nc.vector.tensor_copy(lncol[:, n], lncols[:, ds(layer * 8 + n * 16, 8)])
                last.then_inc(param_ready, 1)
                dve.wait_ge(param_ready, layer + 1)
                norm(0)
                for u in range(3):
                    split_unit(u, u)
                norm_lo("n1", S_N1, 0)
                split_unit(3, 3)
                with dve.Fori(0, 3) as i:
                    for n in (1, 2):
                        for u in range(4):
                            split_unit(4 * n + u, u, more=i * 8)
                for u in range(4):
                    split_unit(28 + u, u, MIX - 7 * COL)
                gate_units = iter(range(32, 56))

                def gate(count=1):
                    for _ in range(count):
                        u = next(gate_units)
                        split_unit(u, u % RING)

                gate(2)

                def rope_heads(src, dst, heads, width, cos, sin):
                    hw = width // 2
                    tmp = scr[:, 0:T * heads * width].rearrange("p (t h d) -> p t h d", t=T, h=heads)
                    cos = cos.rearrange("p (t d) -> p t d", t=T)
                    sin = sin.rearrange("p (t d) -> p t d", t=T)
                    nc.vector.tensor_tensor(dst, src, cos.unsqueeze(2).broadcast_to([P, T, heads, width]), ALU.mult)
                    for a in range(2):
                        b = 1 - a
                        last = nc.vector.tensor_tensor(
                            tmp[:, :, :, hw * a:hw * a + hw], src[:, :, :, hw * b:hw * b + hw],
                            sin[:, :, hw * a:hw * a + hw].unsqueeze(2).broadcast_to([P, T, heads, hw]), ALU.mult)
                    after(link(last))
                    after(link(nc.vector.tensor_tensor(dst, dst, tmp, ALU.add)))

                dve.wait_ge(z_ready, layer * 14 + 9)
                dve.wait_ge(gain_in, layer * 96 + 96)
                nc.vector.tensor_scalar(iw[:], z[:, :, IW:IW + IH], (ID * IH) ** -0.5, None, ALU.mult)
                after(link(nc.vector.tensor_tensor(fbias[:, 0], z[:, :, FF_:FF_ + H],
                                                   gain[:, G_B:G_B + H].unsqueeze(1).broadcast_to([P, T, H]), ALU.add)))
                nc.vector.scalar_tensor_tensor(fbias[:, 1], fbias[:, 0], -1.0, fbias[:, 0],
                                               ALU.mult, ALU.min).then_inc(f_abs, 1)
                zi = z[:, :, IQ:IQ + 9 * ID].rearrange("p t (h d) -> p t h d", d=ID)
                ti = tq[:, :, 0:TQ_DSA].rearrange("p t (h d) -> p t h d", d=ID)
                rope_heads(zi, ti[:, :, 0:9], 9, ID, rope[:, R_COS32:R_SIN32], rope[:, R_SIN32:R_DECAY])
                nc.vector.tensor_copy(ti[:, :, 9:12], ti[:, :, 8:9].broadcast_to([P, T, 3, ID])).then_inc(roped, 1)
                gate(1)
                dve.wait_ge(heads_squared, layer + 1)
                for t in range(T):
                    nc.vector.tensor_reduce(ssq[:, t, 0:2 * H], qa[:, t, :, 0:HD], AX.X, ALU.add)
                nc.vector.tensor_reduce(ssq[:, :, 2 * H:], tq[:, :, TQ_DSA:TQ_DSA + 9 * HD]
                                        .rearrange("p t (h d) -> p t h d", d=HD), AX.X, ALU.add).then_inc(heads_ssq, 1)
                gate(1)
                dve.wait_ge(f_ln, layer + 1)
                nc.vector.scalar_tensor_tensor(lf[:], fbias[:, 0], 0.0, fbias[:, 3], ALU.min, ALU.subtract)\
                    .then_inc(f_lf, 1)
                gate(1)
                dve.wait_ge(heads_rstd, layer + 1)
                zd = z[:, :, DQ:DQ + 9 * HD].rearrange("p t (h d) -> p t h d", d=HD)
                td = tq[:, :, TQ_DSA:TQ_RET].rearrange("p t (h d) -> p t h d", d=HD)
                after(link(nc.vector.tensor_tensor(zd, zd, ssq[:, :, 2 * H:].unsqueeze(3)
                                                   .broadcast_to([P, T, 9, HD]), ALU.mult)))
                for t in range(T):
                    nc.vector.tensor_tensor(zd[:, t, 0:8], zd[:, t, 0:8], gain[:, G_DQ:G_DQ + HD].unsqueeze(1)
                                            .broadcast_to([P, 8, HD]), ALU.mult)
                after(link(nc.vector.tensor_tensor(zd[:, :, 8], zd[:, :, 8], gain[:, G_DK:G_DK + HD].unsqueeze(1)
                                                   .broadcast_to([P, T, HD]), ALU.mult)))
                rope_heads(zd, td[:, :, 0:9], 9, HD, rope[:, R_COS64:R_SIN64], rope[:, R_SIN64:R_COS32])
                nc.vector.tensor_copy(td[:, :, 9], td[:, :, 8]).then_inc(roped, 1)
                gate(1)
                zf = z[:, :, 0:2 * H * HD].rearrange("p t (h d) -> p t h d", d=HD)
                after(link(nc.vector.tensor_tensor(zf, zf, ssq[:, :, 0:2 * H].unsqueeze(3)
                                                   .broadcast_to([P, T, 2 * H, HD]), ALU.mult)))
                for t in range(T):
                    nc.vector.tensor_tensor(
                        qa[:, t, :, 0:HD].rearrange("p (g h) d -> p g h d", g=2),
                        zf[:, t].rearrange("p (g h) d -> p g h d", g=2),
                        gain[:, G_FQ:G_FQ + 2 * HD].rearrange("p (g d) -> p g d", g=2).unsqueeze(2)
                        .broadcast_to([P, 2, H, HD]), ALU.mult)
                nc.vector.memset(qa[:, :, 0:H, HD + 1:HD + 2], 1.0)
                nc.vector.memset(qa[:, :, H:2 * H, HD:HD + 1], 1.0)
                dve.wait_ge(*full_at(layer, "cum", 0))
                c = bank("cum", 0)[:, 0:T * H].rearrange("p (t h) -> p t h", t=T)
                nc.vector.tensor_copy(qa[:, :, 0:H, HD], c)
                nc.vector.tensor_scalar(qa[:, :, H:2 * H, HD + 1], c, -1.0, None, ALU.mult).then_inc(qa_ready, 1)
                gate(2)
                for h in range(IH):
                    dve.wait_ge(rel_ready, layer * IH + h + 1)
                    for t in range(T):
                        c = slice(0, P) if t == 0 else slice(P, 3 * P)
                        if h:
                            dve.wait_ge(scored, layer * 2 * IH + 2 * h - 1 + t)
                        before = con[:, C_MASK + P * (1 - t):C1_COLS] if h == 0 else score[:, c]
                        nc.vector.scalar_tensor_tensor(score[:, c], rel[:, h % 2, c], iw[:, t, h:h + 1], before,
                                                       ALU.mult, ALU.add).then_inc(scored, 1)
                    if h % 2:
                        gate(1)

                def fox_k(hp):
                    dve.wait_ge(*full_at(layer, "fk", hp))
                    nc.vector.tensor_copy(fT[:, hp % 2, 1], bank("fk", hp)[0:HD + 2, :]
                                          .rearrange("p (h s) -> p h s", h=2)).then_inc(fk_ready, 1)

                def scores(kind, h):
                    k = "fd".index(kind)
                    dve.wait_ge(*full_at(layer, kind + "s", h))
                    if k or h >= 2:
                        dve.wait_ge(*full_at(layer, "fd"[(k * H + h - 2) // H] + "p", (h - 2) % H))
                    own_wait(dve)
                    for t in range(T):
                        c = slice(0, P) if t == 0 else slice(P, 3 * P)
                        bias = score[:, c] if k else con[:, C_MASK + P * (1 - t):C1_COLS]
                        last = nc.vector.tensor_tensor_reduce(
                            out=prob[:, h % 2, c], in0=bank(kind + "s", h)[:, c], in1=bias, scale=-1.0, scalar=3e38,
                            op0=ALU.add, op1=ALU.min, accum_out=nmax[:, k, h, t:t + 1])
                    last.then_inc(s_ready, 1)

                def heads_out(kind, g):
                    k = "fd".index(kind)
                    dve.wait_ge(p_ready, layer * 2 * H + k * H + 4 * g + 4)
                    after(link(nc.vector.reciprocal(rinv[:, k, :, 4 * g:4 * g + 4], rsum[:, k, :, 4 * g:4 * g + 4])))
                    dve.wait_ge(*full_at(layer, kind + "o", g))
                    o = bank(kind + "o", g).rearrange("p (t h d) -> p t h d", t=T, h=4)
                    col = k * COL + g * 256
                    nc.vector.tensor_tensor(y[:, :, col:col + 256].rearrange("p t (h d) -> p t h d", h=4), o,
                                            rinv[:, k, :, 4 * g:4 * g + 4].unsqueeze(3).broadcast_to([P, T, 4, HD]),
                                            ALU.mult).then_inc(y_ready, 1)

                found, picked = [0, 0], [0, 0]
                for r in range(TOPK // 8):
                    for t in range(T):
                        c = slice(0, P) if t == 0 else slice(P, 3 * P)
                        if r == 0:
                            dve.wait_ge(scored, layer * 2 * IH + 2 * IH - 1 + t)
                        else:
                            after(picked[t])
                        own_wait(dve)
                        found[t] = link(nc.vector.max(top8[:, t], score[:, c]))
                    for t in range(T):
                        c = slice(0, P) if t == 0 else slice(P, 3 * P)
                        after(found[t])
                        own_wait(dve)
                        picked[t] = link(nc.vector.match_replace(score[:, c], top8[:, t], score[:, c], TAKEN))
                after(picked[1])
                after(link(nc.vector.tensor_scalar(score[:], score[:], TAKEN_CUT, NEG, ALU.is_gt, ALU.mult)))
                for t in range(T):
                    c = slice(2 * P * t, 2 * P * t + P)
                    n = link(nc.vector.tensor_tensor(score[:, c], score[:, c], con[:, C_MASK + P:C1_COLS], ALU.add))
                after(n)
                gate(2)
                for h in range(H):
                    if h % 2 == 0:
                        fox_k(h // 2)
                    scores("f", h)
                    gate(1)
                    if h == 5:
                        heads_out("f", 0)
                for h in range(H):
                    scores("d", h)
                    if h == 1:
                        heads_out("f", 1)
                    if h < 2:
                        gate(1)
                    if h == 5:
                        heads_out("d", 0)
                heads_out("d", 1)
                assert next(gate_units, None) is None
                for h in range(RH):
                    dve.wait_ge(*full_at(layer, "rs", h))
                    if h < 2:
                        dve.wait_ge(*full_at(layer, "dp", 6 + h))
                    else:
                        dve.wait_ge(*full_at(layer, "ro", 0))
                    nc.vector.tensor_tensor(prob[:, h % 2], bank("rs", h)[:, 0:3 * P],
                                            rope[:, R_DECAY + 3 * P * h:R_DECAY + 3 * P * (h + 1)],
                                            ALU.mult).then_inc(at_ready, 1)
                dve.wait_ge(ret_rstd, layer + 1)
                yr = y[:, :, D:D + COL]
                yr4 = yr.rearrange("p t (h d) -> p t h d", h=RH)
                after(link(nc.vector.tensor_tensor(yr4, yr4, rssq[:].unsqueeze(3).broadcast_to([P, T, RH, RV]), ALU.mult)))
                dve.wait_ge(ret_gate, layer + 1)
                nc.vector.tensor_tensor(yr, yr, sig_rg, ALU.mult).then_inc(y_ready, 1)
                for j in range(6):
                    split_transposed("yt", j, S_YT + j, hT_hi[:, 2 * j:2 * j + 2], hT_lo[:, 2 * j:2 * j + 2])
                units = iter(range(U_BR, U_WO + 2))
                for n in range(4):
                    u = next(units)
                    split_unit(u, u % RING)
                dve.wait_ge(gates_ready, layer + 1)
                for ct in range(2):
                    for b in range(3):
                        n = 3 * ct + b
                        dve.wait_ge(*tile_done(layer, 14 + n))
                        cols = slice(ct * COL, (ct + 1) * COL)
                        for t in range(T):
                            last = nc.vector.tensor_tensor(nrm[:, t, cols] if b == 0 else gated[:, t],
                                                           acc[:, 2 * (n % 2) + t],
                                                           gates[:, t, b * D + ct * COL:b * D + (ct + 1) * COL], ALU.mult)
                        last.then_inc(branch_taken, 1)
                        if b:
                            dve.wait_ge(branch_taken, layer * 6 + n + 1)
                            for t in range(T):
                                last = nc.vector.tensor_tensor(nrm[:, t, cols], nrm[:, t, cols], gated[:, t], ALU.add)
                            if b == 2:
                                last.then_inc(merged, 1)
                            else:
                                after(link(last))
                        for _ in range(2):
                            u = next(units, None)
                            if u is not None:
                                split_unit(u, u % RING)
                for j in range(4):
                    split_transposed("mg", j, S_MG + j, act_hi[:, 2 * j:2 * j + 2], act_lo[:, 2 * j:2 * j + 2])
                for u in range(2, 6):
                    split_unit(U_WO + u, u % RING)

                def add_x(tile, ct):
                    dve.wait_ge(*tile_done(layer, tile))
                    for t in range(T):
                        cols = slice(ct * COL, (ct + 1) * COL)
                        nc.vector.tensor_tensor(x_sb[:, t, cols], x_sb[:, t, cols], acc[:, 2 * (tile % 2) + t],
                                                ALU.add).then_inc(resid, 1)

                add_x(20, 0)
                for u in range(6, 8):
                    split_unit(U_WO + u, u % RING)
                add_x(21, 1)
                for u in range(3):
                    split_unit(U_FI + u, u)
                norm(1)
                norm_lo("n2", S_N2, 1)
                split_unit(U_FI + 3, 3)

                def gate_up(n, b, more=0):
                    dve.wait_ge(silu_ready, layer * FF_TILES + more + n + 1)
                    for t in range(T):
                        last = nc.vector.tensor_tensor(hid[:, b, t], hid[:, b, t], acc[:, 2 * b + t, 256:512], ALU.mult)
                    last.then_inc(hid_ready, 1)

                with dve.Fori(0, 5) as i:
                    for n in (1, 2):
                        for u in range(4):
                            split_unit(U_FI + 4 * n + u, u, more=i * 8)
                            if u == 1:
                                gate_up(n - 1, 1 - n % 2, i * 2)
                        b, k = PLAN["hid", n - 1]
                        dve.wait_ge(tr_hi, layer * SPLITS + i * 2 + S_HID + n)
                        kt = ds(i * 4 + 2 * (n - 1), 2)
                        nc.vector.tensor_tensor(hT_lo[:, kt], small[:, b].rearrange("p (k s) -> p k s", k=2),
                                                hT_hi[:, kt].bitcast(f32), ALU.subtract).then_inc(tr_split, 1)
                gate_up(10, 0)
                for u in range(3):
                    split_unit(U_FO + u, u)
                split_transposed("hid", 10, S_HID + 10, hT_hi[:, 20:22], hT_lo[:, 20:22])
                for u in range(3, 24):
                    split_unit(U_FO + u, u % RING, k=2 if u % 12 < 10 else 1)
                    if u == 15:
                        add_x(33, 0)
                add_x(34, 1)
                assert links[0] == DVE_LINKS, links

        @block.tensor
        def _(pe):
            pe.sem_inc(used, RING)
            ident = con[:, C_ID:C_ID + P]
            pe.wait_ge(consts_in, 64)
            nc.tensor.transpose(small[:, 0, 0:32], lnrows[:], con[0:32, C_ID:C_ID + 32]).then_inc(ln_tp, 1)

            with pe.Fori(0, DEPTH) as layer:
                def multiply(u, tile, kt, hi, lo, first, last, cols=COL, k=2, more=0):
                    slot = u % RING
                    pe.wait_ge(split, layer * UNITS + more + RING + u + 1)
                    for kk in range(k):
                        for j, (a, w) in enumerate(((hi, w_hi), (lo, w_hi), (hi, w_lo))):
                            for t in range(T):
                                mm = nc.tensor.matmul(acc[:, 2 * (tile % 2) + t, 0:cols],
                                                      a[:, kt + kk, t * P:(t + 1) * P], w[:, slot, kk, 0:cols],
                                                      start=first and kk == 0 and j == 0,
                                                      stop=last and kk == k - 1 and j == 2)
                    mm.then_inc(used, 1)

                def transposed(name, j, src, free=True):
                    if free:
                        pe.wait_ge(*bank_free(layer, name, j))
                    for kk in range(2):
                        for t in range(T):
                            c = kk * SEQ + t * P
                            last = nc.tensor.transpose(bank(name, j)[:, c:c + P],
                                                       src[:, t, kk * P:(kk + 1) * P], ident)
                    last.then_inc(small_full[PLAN[name, j][0]], 1)

                pe.wait_ge(x_normed, 2 * layer + 1)
                for j in range(4):
                    transposed("n1", j, nrm[:, :, 2 * P * j:2 * P * (j + 1)], free=False)
                for u in range(4):
                    pe.wait_ge(tr_split, layer * SPLITS + S_N1 + u + 1)
                    multiply(u, 0, 2 * u, act_hi, act_lo, u == 0, u == 3)
                with pe.Fori(0, 3) as i:
                    for n in (1, 2):
                        pe.wait_ge(z_ready, layer * 14 + i * 2 + n)
                        for u in range(4):
                            multiply(4 * n + u, n, 2 * u, act_hi, act_lo, u == 0, u == 3, more=i * 8)
                pe.wait_ge(z_ready, layer * 14 + 7)
                for u in range(4):
                    multiply(28 + u, 7, 2 * u, act_hi, act_lo, u == 0, u == 3, MIX - 7 * COL)
                gate_units = iter(range(32, 56))

                def gate(count=1):
                    for _ in range(count):
                        u = next(gate_units)
                        if u % 4 == 0:
                            pe.wait_ge(z_ready, layer * 14 + u // 4)
                        multiply(u, u // 4, 2 * (u % 4), act_hi, act_lo, u % 4 == 0, u % 4 == 3)

                def roped_T(j):
                    if j < 5:
                        pe.wait_ge(roped, layer * 2 + (1 if j < 2 else 2))
                    else:
                        pe.wait_ge(ret_roped, layer + 1)
                    pe.wait_ge(*bank_free(layer, "t", j))
                    for n, b in enumerate(T_BLOCKS[j]):
                        for t in range(T):
                            c = n * SEQ + t * P
                            last = nc.tensor.transpose(bank("t", j)[:, c:c + P], tq[:, t, b * P:(b + 1) * P], ident)
                    last.then_inc(small_full[PLAN["t", j][0]], 1)

                def scores(name, j, q, k):
                    nc.tensor.matmul(bank(name, j)[:, 0:P], q[:, 0:P], k[:, 0:P], start=True, stop=True)
                    nc.tensor.matmul(bank(name, j)[:, P:3 * P], q[:, P:SEQ], k[:, 0:SEQ], start=True, stop=True) \
                        .then_inc(small_full[PLAN[name, j][0]], 1)

                gate(4)
                roped_T(0)
                roped_T(1)
                pe.wait_ge(f_lf, layer + 1)
                pe.wait_ge(*bank_free(layer, "cum", 0))
                upto, ones = con[:, C_UPTO:C_UPTO + P], con[:, C_ONES:C_ONES + P]
                c = bank("cum", 0)
                nc.tensor.matmul(c[:, 0:H], upto, lf[:, 0], start=True, stop=True)
                nc.tensor.matmul(c[:, H:2 * H], ones, lf[:, 0], start=True, stop=False)
                nc.tensor.matmul(c[:, H:2 * H], upto, lf[:, 1], start=False, stop=True) \
                    .then_inc(small_full[PLAN["cum", 0][0]], 1)
                gate(4)
                pe.wait_ge(t_ready, layer * 7 + 2)
                for h in range(IH):
                    r = slice(ID * (h % 4), ID * (h % 4) + ID)
                    pe.wait_ge(*bank_free(layer, "idx", h))
                    scores("idx", h, tT[r, h // 4], tT[r, B_IK])
                    if h % 2 and h > 1:
                        gate(1)
                for j in range(2, 7):
                    roped_T(j)
                gate(3)

                def fox_T(hp):
                    pe.wait_ge(qa_ready, layer + 1)
                    for g, name in enumerate(("fq", "fk")):
                        pe.wait_ge(*bank_free(layer, name, hp))
                        for n in range(2):
                            for t in range(T):
                                c = n * SEQ + t * P
                                last = nc.tensor.transpose(bank(name, hp)[0:HD + 2, c:c + P],
                                                           qa[:, t, g * H + 2 * hp + n], ident)
                        last.then_inc(small_full[PLAN[name, hp][0]], 1)

                def head_scores(kind, h):
                    if kind == "f":
                        if h % 2 == 0:
                            fox_T(h // 2)
                            pe.wait_ge(fq_ready, layer * 4 + h // 2 + 1)
                            pe.wait_ge(fk_ready, layer * 4 + h // 2 + 1)
                        f = fT[:, h // 2 % 2]
                        q, k = f[:, 0, h % 2], f[:, 1, h % 2]
                    else:
                        r = slice(HD * (h % 2), HD * (h % 2) + HD)
                        q, k = tT[r, B_DQ + h // 2], tT[r, B_DK]
                        if h == 0:
                            pe.wait_ge(t_ready, layer * 7 + 7)
                    pe.wait_ge(*bank_free(layer, kind + "s", h))
                    scores(kind + "s", h, q, k)

                def probs_T(kind, h):
                    pe.wait_ge(p_ready, layer * 2 * H + "fd".index(kind) * H + h + 1)
                    pe.wait_ge(*bank_free(layer, kind + "p", h))
                    for n in range(3):
                        last = nc.tensor.transpose(bank(kind + "p", h)[:, n * P:(n + 1) * P],
                                                   prob[:, h % 2, n * P:(n + 1) * P], ident)
                    last.then_inc(small_full[PLAN[kind + "p", h][0]], 1)

                def weighted(o, pT, v0, v1):
                    nc.tensor.matmul(o[0], pT[:, 0:P], v0, start=True, stop=True)
                    nc.tensor.matmul(o[1], pT[:, P:2 * P], v0, start=True, stop=False)
                    return nc.tensor.matmul(o[1], pT[:, 2 * P:3 * P], v1, start=False, stop=True)

                def head_out(kind, h):
                    k = "fd".index(kind)
                    pe.wait_ge(pT_ready, layer * 2 * H + k * H + h + 1)
                    name, g = kind + "o", h // 4
                    if h % 4 == 0:
                        pe.wait_ge(*bank_free(layer, name, g))
                    o = bank(name, g).rearrange("p (t h d) -> p t h d", t=T, h=4)
                    v = DV if k else FV + HD * h
                    last = weighted([o[:, t, h % 4] for t in range(T)], probT[:, h % 2],
                                    z[:, 0, v:v + HD], z[:, 1, v:v + HD])
                    if h % 4 == 3:
                        last.then_inc(small_full[PLAN[name, g][0]], 1)

                heads = [(kind, h) for kind in "fd" for h in range(H)]
                head_scores(*heads[0])
                for n, (kind, h) in enumerate(heads):
                    if n + 1 < len(heads):
                        head_scores(*heads[n + 1])
                    probs_T(kind, h)
                    if n < 10:
                        gate(1)
                    head_out(kind, h)
                assert next(gate_units, None) is None

                for r in range(2):
                    for h in (2 * r, 2 * r + 1):
                        rows = slice(HD * (h % 2), HD * (h % 2) + HD)
                        q, k = tT[rows, B_RQ + h // 2], tT[rows, B_RK + h // 2]
                        pe.wait_ge(*bank_free(layer, "rs", h))
                        s = bank("rs", h)
                        nc.tensor.matmul(s[:, 0:SEQ], k[:, 0:P], q, start=True, stop=True)
                        nc.tensor.matmul(s[:, SEQ:3 * P], k[:, P:SEQ], q[:, P:SEQ], start=True, stop=True) \
                            .then_inc(small_full[PLAN["rs", h][0]], 1)
                    pe.wait_ge(*bank_free(layer, "ro", r))
                    o = bank("ro", r).rearrange("p (t h d) -> p t h d", t=T, h=2)
                    for h in (2 * r, 2 * r + 1):
                        pe.wait_ge(at_ready, layer * RH + h + 1)
                        v = slice(RVC + RV * h, RVC + RV * (h + 1))
                        last = weighted([o[:, t, h % 2] for t in range(T)], prob[:, h % 2], z[:, 0, v], z[:, 1, v])
                    last.then_inc(small_full[PLAN["ro", r][0]], 1)

                for j in range(6):
                    pe.wait_ge(y_ready, layer * 5 + (2, 2, 4, 4, 5, 5)[j])
                    transposed("yt", j, y[:, :, 2 * P * j:2 * P * (j + 1)])
                for n in range(6):
                    b = n % 3
                    if n < 2:
                        pe.wait_ge(z_ready, layer * 14 + 13 + n + 1)
                    else:
                        pe.wait_ge(branch_taken, layer * 6 + n - 1)
                    for u in range(2):
                        pe.wait_ge(tr_split, layer * SPLITS + S_YT + 2 * b + u + 1)
                        multiply(U_BR + 2 * n + u, 14 + n, 4 * b + 2 * u, hT_hi, hT_lo, u == 0, u == 1)
                for j in range(4):
                    pe.wait_ge(merged, layer * 2 + j // 2 + 1)
                    transposed("mg", j, nrm[:, :, 2 * P * j:2 * P * (j + 1)])
                for ct in range(2):
                    pe.wait_ge(branch_taken, layer * 6 + 5 + ct)
                    for u in range(4):
                        pe.wait_ge(tr_split, layer * SPLITS + S_MG + u + 1)
                        multiply(U_WO + 4 * ct + u, 20 + ct, 2 * u, act_hi, act_lo, u == 0, u == 3)

                pe.wait_ge(x_normed, 2 * layer + 2)
                for j in range(4):
                    transposed("n2", j, nrm[:, :, 2 * P * j:2 * P * (j + 1)])

                def ff_tile(n, i=0):
                    for u in range(4):
                        if n == 0:
                            pe.wait_ge(tr_split, layer * SPLITS + S_N2 + u + 1)
                        if u == 3 and n:
                            pe.wait_ge(hid_ready, layer * FF_TILES + i * 2 + n + 1)
                            b = PLAN["hid", n - 1][0]
                            pe.wait_ge(tr_split, layer * SPLITS + i * 2 + S_HID + n - 2)
                            hidden_T(b, 1 - n % 2)
                        multiply(U_FI + 4 * n + u, 22 + n, 2 * u, act_hi, act_lo, u == 0, u == 3, more=i * 8)

                def hidden_T(b, buf):
                    for kk in range(2):
                        for t in range(T):
                            c = kk * SEQ + t * P
                            last = nc.tensor.transpose(small[:, b, c:c + P], hid[:, buf, t, kk * P:(kk + 1) * P], ident)
                    last.then_inc(small_full[b], 1)

                ff_tile(0)
                with pe.Fori(0, 5) as i:
                    for n in (1, 2):
                        pe.wait_ge(hid_ready, layer * FF_TILES + i * 2 + n)
                        ff_tile(n, i)
                for ct in range(2):
                    pe.wait_ge(hid_ready, layer * FF_TILES + 11 + ct)
                    for u in range(12):
                        if ct == 0:
                            if u == 3:
                                pe.wait_ge(tr_split, layer * SPLITS + S_HID + 9)
                                hidden_T(PLAN["hid", 10][0], 0)
                            pe.wait_ge(tr_split, layer * SPLITS + S_HID + min(u, 10) + 1)
                        k = 2 if u < 10 else 1
                        multiply(U_FO + 12 * ct + u, 33 + ct, 2 * u if u < 11 else 21, hT_hi, hT_lo, u == 0, u == 11, k=k)


_INS = ("x", "w_in", "w_fox_out", "w_dsa_out", "w_ret_out", "w_o", "w_ffn_in", "w_ffn_out", "ln1_g", "ln2_g",
        "fox_b_f", "fox_q_norm", "fox_k_norm", "dsa_q_norm", "dsa_k_norm", "ret_out_norm")


def kernel(**inputs):
    import concourse.bacc as bacc
    from concourse.bass_utils import run_bass_kernel_spmd

    nc = bacc.Bacc("TRN2", target_bir_lowering=False, num_devices=1)
    arrays = {f"{n}_dram": np.ascontiguousarray(inputs[n]) for n in _INS}
    for n, table in enumerate(rope_and_masks()):
        arrays[f"table{n + 1}_dram"] = table
    aps = [nc.dram_tensor(n, a.shape, mybir.dt.float32, kind="ExternalInput").ap() for n, a in arrays.items()]
    out = nc.dram_tensor("out_dram", (1, SEQ, D), mybir.dt.float32, kind="ExternalOutput").ap()
    build(nc, *aps, out)
    return run_bass_kernel_spmd(nc, [arrays], core_ids=[0]).results[0]["out_dram"]
```

```python
import numpy as np
import concourse.bass as bass
from concourse import mybir
from contextlib import ExitStack

D, SEQ, DEPTH, P = 1024, 256, 2, 128
T = SEQ // P
H, HD, IH, ID, RH, RV = 8, 64, 8, 32, 4, 128
FF = 2816
TOPK = 64
EPS = 1e-6
FV, ZB, DQ, DV, IQ, IW = 1024, 1536, 1544, 2120, 2184, 2472
ZC, RQ, RVC, RG, ZG = 2480, 2480, 2992, 3504, 4016
IN_COLS = ZG + 3 * D
NEG, TAKEN, TAKEN_CUT = -1e30, -3e38, -2e38

COL = 512
RING = 4
FF_TILES = FF // 256
LEAD = 3
TILE_COLS = (1536, 2048, 0, 512, 1024, 2560, 3072, 3584) + tuple(range(ZG, IN_COLS, COL))
NARROW = 7
U_BR, U_WO, U_FI, U_FO, UNITS = 56, 68, 76, 120, 144
SLOT_UNITS = UNITS // RING
BRANCH_GATE = (1, 0, 2)
WO_UNITS = ((0, 0), (0, 1), (1, 0), (1, 1), (0, 2), (0, 3), (1, 2), (1, 3))


def rope_and_masks():
    f = np.float32
    pos = np.arange(SEQ, dtype=f)

    def rope(half):
        inv = (f(10000.0) ** (-np.arange(half, dtype=f) / f(half))).astype(f)
        ang = (pos[:, None] * inv[None]).astype(f).astype(np.float64)
        c, s = np.cos(ang).astype(f), np.sin(ang).astype(f)
        both = np.concatenate([c, c, -s, s], 1)
        return both.reshape(T, P, 2, 2 * half).transpose(1, 2, 0, 3).reshape(P, -1)

    i = np.arange(P)
    causal = np.where(i[None] <= i[:, None], 0.0, NEG)
    mask = np.concatenate([np.zeros((P, P)), causal], 1)
    upto = (i[:, None] <= i[None]).astype(f)
    log_g = np.log1p(-(2.0 ** (-5.0 - np.arange(RH))))
    diff = np.arange(2 * P)[None] - i[:, None]
    dec = [np.where(diff >= 0, np.exp(np.maximum(diff, 0) * g), 0) * RETQK_SCALE for g in log_g]
    decay = np.concatenate([np.concatenate([d, d[:, :P]], 1) for d in dec], 1)
    return [np.ascontiguousarray(a.astype(f)) for a in (
        np.concatenate([np.eye(P), upto, np.ones((P, P)), mask], 1),
        np.concatenate([rope(HD // 2), rope(ID // 2), decay], 1))]


RETQK_SCALE = 64 ** -0.5
C_ID, C_UPTO, C_ONES, C_MASK, C1_COLS = 0, 128, 256, 384, 640
R_COS64, R_SIN64, R_COS32, R_SIN32, R_DECAY = 0, 128, 256, 320, 384
C2_COLS = R_DECAY + RH * 3 * P
G_FQ, G_FK, G_DQ, G_DK, G_RET, G_B, G_COLS = 0, 64, 128, 192, 256, 768, 776
TQ_DSA, TQ_RET, TQ_COLS = 384, 1024, 1536
T_BLOCKS = [(0, 1), (2,), (3, 4), (5, 6), (7,), (8, 9), (10, 11)]
B_IK, B_DQ, B_DK, B_RQ, B_RK = 2, 3, 7, 8, 10

S_N1, S_YT, S_MG, S_N2, S_HID, SPLITS = 0, 4, 10, 14, 18, 29


def tile_width(tile):
    return ZG - TILE_COLS[tile] if tile == NARROW else COL


def schedule():
    steps, units = [], iter(range(U_FI + 4))

    def unit(count=1):
        for _ in range(count):
            u = next(units)
            if u in (U_WO - 2, U_WO):
                steps.append(("branch", (u - U_BR) // 2 - 1))
            if u % 4 == 1 and 32 < u - 1 < U_BR:
                steps.append(("evac", u // 4 - 1))
            steps.append(("unit", u))
            if u % 4 == 0 and (4 <= u <= 32 or u == U_BR):
                steps.append(("evac", u // 4 - 1))
            if U_BR + 2 <= u < U_WO - 2 and u % 2 == 0:
                steps.append(("branch", (u - U_BR) // 2 - 1))

    def add(*more):
        steps.extend(more)

    add(("n1", 0), ("lead", 0), ("n1", 1), ("lead", 1), ("lead", 2))
    unit()
    add(("n1", 2), ("n1", 3), ("rms", 0))
    unit(8)
    add(("forget", 0), ("irope", 0))
    unit()
    add(("dsums", 0))
    unit()
    add(("t", 0), ("t", 1))
    unit()
    add(("cum", 0), ("idx", 0), ("idx", 1))
    unit()
    add(("cum_out", 0), ("dnorm", 0), ("idx", 2))
    unit()
    add(("idx", 3), ("idx", 4))
    unit()
    add(("drope", 0))
    unit()
    add(("idx", 5), ("idx", 6))
    unit()
    add(("idx", 7), ("t", 2), ("t", 3), ("t", 4))
    unit()
    add(("fsquares", 0), ("pick", 0))
    unit()
    add(("pick", 1))
    unit()
    add(("fsums", 0))
    unit()
    add(("pick", 2))
    unit()
    add(("pick", 3))
    unit()
    add(("fnorm", 0))
    unit(2)
    for r in range(4, 8):
        add(("pick", r))
        unit()
    add(("picked", 0))
    unit()
    add(("ds", 0))
    unit()

    for h in range(H):
        add(("dp", h))
        if h < H - 1:
            add(("ds", h + 1))
        if h == 4:
            add(("heads_out", 0))
        unit()
        add(("do", h))
    add(("heads_out", 1), ("t", 5), ("t", 6))
    unit()
    add(("rs", 0), ("rs", 1))
    unit()
    add(("ro", 0), ("ro", 1), ("rs", 2), ("rs", 3))
    unit()
    add(("ro", 2), ("ro", 3))
    unit()
    add(("fT", 0), ("yt", 0))
    unit()
    add(("yt", 1), ("fs", 0))
    unit()
    for h in range(0, H, 2):
        add(("fp", h), ("fs", h + 1))
        if h == 4:
            add(("heads_out", 2))
        unit()
        if h < H - 2:
            add(("fT", h // 2 + 1))
        add(("fo", h), ("fp", h + 1))
        unit()
        if h < H - 2:
            add(("fs", h + 2), ("fo", h + 1))
            unit()
        else:
            add(("fo", h + 1))
    add(("sig_rg", 0))
    unit()
    add(("heads_out", 3), ("sigmoid", 10))
    unit()
    add(("yt", 2), ("yt", 3), ("sigmoid", 11))
    unit(2)
    add(("sigmoid", 8))
    unit()
    add(("yt", 4), ("yt", 5), ("sigmoid", 9))
    unit()
    add(("sigmoid", 12))
    while steps[-1] != ("unit", U_WO - 2):
        unit()
    add(("mg", 0), ("mg", 1))
    unit(3)
    add(("mg", 2), ("mg", 3))
    unit(4)
    add(("add_x", 0))
    unit()
    add(("n2", 0), ("n2", 1))
    unit()
    add(("add_x", 1))
    unit()
    add(("n2", 2), ("n2", 3), ("rms", 1))
    unit(3)
    assert next(units, None) is None and sum(8 for name, _ in steps if name == "pick") == TOPK
    return steps


def small_bank_plan(steps):
    order = []
    for name, n in steps:
        if name in ("n1", "n2", "mg", "yt"):
            order.append((name, n, n % 4 if name != "yt" else 2 + n % 2))
        elif name == "t":
            order.append((name, n, (0, 1, 2, 3, 2, 2, 0)[n]))
        elif name == "cum":
            order.append((name, n, 2))
        elif name in ("idx", "ds", "fs", "rs"):
            order.append((name, n, n % 2))
        elif name in ("dp", "fp"):
            order.append((name, n, 2))
        elif name in ("do", "fo") and n % 4 == 0:
            order.append((name, n // 4, 3))
        elif name == "ro" and n % 2 == 0:
            order.append((name, n // 2, 3))
        elif name == "fT":
            order += [("fq", n, 0), ("fk", n, 1)]
    order += [("hid", n, 2 + n % 2) for n in range(FF_TILES)]
    uses, plan = [0] * 4, {}
    for name, n, bank in order:
        plan[name, n] = (bank, uses[bank])
        uses[bank] += 1
    return plan, uses


SCHEDULE = schedule()
PLAN, BANK_USES = small_bank_plan(SCHEDULE)


def last_unit(tile):
    if tile < 14:
        return 4 * tile + 3
    if tile < 20:
        return U_BR + 2 * (tile - 14) + 1
    if tile < 22:
        return U_WO + (5, 7)[tile - 20]
    if tile < 33:
        return U_FI + 4 * (tile - 22) + 3
    return U_FO + 12 * (tile - 33) + 11


DVE_LINKS, POOL_LINKS = 49, 12


def build(nc, x, w_in, w_fox_out, w_dsa_out, w_ret_out, w_o, w_ffn_in, w_ffn_out,
          ln1_g, ln2_g, fox_b_f, fox_q_norm, fox_k_norm, dsa_q_norm, dsa_k_norm, ret_out_norm,
          table1, table2, out):
    f32, f32r = mybir.dt.float32, mybir.dt.float32r
    ALU, ACT, AX = mybir.AluOpType, mybir.ActivationFunctionType, mybir.AxisListType
    ds = bass.ds
    with ExitStack() as ctx:
        def sb(name, shape, dt=f32):
            return ctx.enter_context(nc.sbuf_tensor(name, shape, dt))

        def sem(name):
            return ctx.enter_context(nc.semaphore(name))

        x_sb = sb("x_sb", [P, T, D])
        nrm = sb("nrm", [P, T, D])
        act_hi = sb("act_hi", [P, 8, SEQ], f32r)
        act_lo = sb("act_lo", [P, 8, SEQ], f32r)
        raw = sb("raw", [P, RING, 2, COL])
        w_hi = sb("w_hi", [P, RING, 2, COL], f32r)
        w_lo = sb("w_lo", [P, RING, 2, COL], f32r)
        con = sb("con", [P, C1_COLS])
        rope = sb("rope", [P, C2_COLS])
        gains = sb("gains", [P, DEPTH, G_COLS])
        gain = sb("gain", [P, G_COLS])
        lnrows = sb("lnrows", [2 * DEPTH * 8, P])
        lncols = sb("lncols", [P, 2 * DEPTH * 8])
        lncol = sb("lncol", [P, 2, 8])
        gates = sb("gates", [P, T, 3 * D])
        tq = sb("tq", [P, T, TQ_COLS])
        y = tq
        qa = sb("qa", [P, T, 2 * H, HD + 2])
        iw = sb("iw", [P, T, IH])
        ssq_f = sb("ssq_f", [P, T, 2 * H])
        ssq_d = sb("ssq_d", [P, T, 9])
        xssq = sb("xssq", [P, T])
        half = sb("half", [P, T * 2 * H])
        fbias = sb("fbias", [P, 4, T, H])
        lf = sb("lf", [P, T, H])
        nmax = sb("nmax", [P, 2, H, T])
        rsum = sb("rsum", [P, 2, T, H])
        rinv = sb("rinv", [P, 2, T, H])
        rssq = sb("rssq", [P, T, RH])
        top8 = sb("top8", [P, 2, 8])
        score = sb("score", [P, 3 * P])
        work = sb("work", [P, 3, 2, 3 * P])
        rel, prob, probT = (work[:, n] for n in range(3))
        hid = work[:, :, :, :].rearrange("p a b c -> p (a b c)")[:, 0:2 * T * 256] \
            .rearrange("p (b t c) -> p b t c", b=2, t=T)
        arena_at = (nc.sbuf_base + 31) // 32 * 32
        arena_words = T * ZG + 12 * SEQ + 8 * SEQ
        sb("arena", [P, arena_words])

        def at(name, shape, word, dt=f32):
            return nc.alloc_sbuf_tensor_at(name, shape, dt, offset=arena_at + 4 * word)

        z_a = at("z_a", [P, T, ZB], 0)
        fT = at("fT", [HD + 2, 2, 2, 2, SEQ], T * ZB)
        tT_at = T * ZB + 8 * SEQ
        tT = at("tT", [P, 12, SEQ], tT_at)
        z_b = at("z_b", [P, T, ZC - ZB], tT_at + 12 * SEQ)
        z_c = at("z_c", [P, T, ZG - ZC], tT_at + 12 * SEQ + T * (ZC - ZB))
        yT = [[at(f"yT{part}{b}", [P, 4, SEQ], word + 4 * SEQ * part, f32r) for part in range(2)]
              for b, word in enumerate((tT_at, 0, T * ZB))]
        hT_hi = at("hT_hi", [P, FF // P, SEQ], 0, f32r)
        hT_lo = at("hT_lo", [P, FF // P, SEQ], FF // P * SEQ, f32r)
        pool_tmp = gates[:, :, 2 * D:2 * D + 2 * RH * HD].rearrange("p t (h d) -> p t h d", h=2 * RH)
        sig_rg = qa[:, :, :, :].rearrange("p t h d -> p (t h d)")[:, 0:T * COL].rearrange("p (t c) -> p t c", t=T)
        gated = qa[:, :, :, :].rearrange("p t h d -> p (t h d)")[:, T * COL:2 * T * COL].rearrange("p (t c) -> p t c", t=T)
        scr = nrm[:, :, :].rearrange("p t c -> p (t c)")

        acc = ctx.enter_context(nc.psum_tensor("acc", [P, 4, COL], f32))
        small = ctx.enter_context(nc.psum_tensor("small", [P, 4, COL], f32))

        first_in = sem("first_in")
        x_in = [sem(f"x_in{n}") for n in range(4)]
        consts_in = sem("consts_in")
        gain_in = sem("gain_in")
        resid = sem("resid")
        loaded = [sem(f"loaded{s}") for s in range(RING)]
        rounded = sem("rounded")
        split = sem("split")
        first_half = sem("first_half")
        used = sem("used")
        z_ready = sem("z_ready")
        branch_taken = sem("branch_taken")
        small_full = [sem(f"small_full{b}") for b in range(4)]
        tr_hi, tr_split = sem("tr_hi"), sem("tr_split")
        x_squared, x_rstd = sem("x_squared"), sem("x_rstd")
        heads_squared, heads_ssq, heads_rstd = sem("heads_squared"), sem("heads_ssq"), sem("heads_rstd")
        ret_copied = sem("ret_copied")
        f_abs, f_ln, f_lf = sem("f_abs"), sem("f_ln"), sem("f_lf")
        cum_taken, qa_ready = sem("cum_taken"), sem("qa_ready")
        roped, ret_roped, t_ready = sem("roped"), sem("ret_roped"), sem("t_ready")
        fq_ready, fk_ready = sem("fq_ready"), sem("fk_ready")
        rel_ready, scored = sem("rel_ready"), sem("scored")
        s_ready, p_ready, pT_ready = sem("s_ready"), sem("p_ready"), sem("pT_ready")
        at_ready, ret_out, ret_rstd = sem("at_ready"), sem("ret_out"), sem("ret_rstd")
        sig_rg_ready, ret_y_ready, gates_ready = sem("sig_rg_ready"), sem("ret_y_ready"), sem("gates_ready")
        y_ready, merged, silu_ready, hid_ready = sem("y_ready"), sem("merged"), sem("silu_ready"), sem("hid_ready")
        param_ready = sem("param_ready")
        dve_order, act_order, pool_order = sem("dve_order"), sem("act_order"), sem("pool_order")
        ln_tp, ln_cols = sem("ln_tp"), sem("ln_cols")
        stored = sem("stored")
        carried = sem("carried")

        def full_at(layer, name, j):
            bank, k = PLAN[name, j]
            return small_full[bank], layer * BANK_USES[bank] + k + 1

        def released(layer, name, j):
            done, per_layer, n = {
                "n1": (tr_split, SPLITS, S_N1 + j), "yt": (tr_split, SPLITS, S_YT + j),
                "mg": (tr_split, SPLITS, S_MG + j), "n2": (tr_split, SPLITS, S_N2 + j),
                "t": (t_ready, 7, j), "cum": (cum_taken, 1, 0), "idx": (rel_ready, IH, j),
                "fq": (fq_ready, 4, j), "fk": (fk_ready, 4, j),
                "ds": (s_ready, 2 * H, j), "fs": (s_ready, 2 * H, H + j),
                "dp": (pT_ready, 2 * H, j), "fp": (pT_ready, 2 * H, H + j),
                "do": (y_ready, 4, j), "fo": (y_ready, 4, 2 + j),
                "rs": (at_ready, RH, j), "ro": (ret_out, 2, j)}[name]
            return done, layer * per_layer + n + 1

        def bank_free(layer, name, j):
            b, k = PLAN[name, j]
            before = next(step for step, place in PLAN.items() if place == (b, k - 1))
            return released(layer, *before)

        def own_wait(eng):
            eng.sem_inc(carried, 1)

        def tile_done(layer, tile, more=0):
            return used, layer * UNITS + more + RING + last_unit(tile) + 1

        def bank(name, j):
            return small[:, PLAN[name, j][0], :]

        def load_x(eng, n):
            c = slice(2 * P * n, 2 * P * (n + 1))
            eng.dma_start(x_sb[:, :, c], x[0, :, c].rearrange("(t p) d -> p t d", p=P)).then_inc(x_in[n], 16)

        block = ctx.enter_context(nc.Block())

        @block.sync
        def _(sp):
            sp.dma_start(con[:, C_ID:C_ID + P], table1[:, C_ID:C_ID + P]).then_inc(first_in, 16)
            for n, g in enumerate((ln1_g, ln2_g)):
                sp.dma_start(lnrows[n * 8 * DEPTH:(n + 1) * 8 * DEPTH, :],
                             g.rearrange("l (k p) -> (l k) p", p=P)).then_inc(first_in, 16)
            load_x(sp, 0)
            load_x(sp, 1)

            def unit(layer, u, slot, dst, src):
                sp.wait_ge(split, layer * UNITS + u + 1)
                if u == 8:
                    own_wait(sp)
                sp.dma_start(dst, src).then_inc(loaded[slot], 16)

            def rows(w, layer, r, col, cols, k=2):
                return w[ds(layer, 1), r * P:(r + k) * P, col:col + cols] \
                    .rearrange("a (k p) n -> p (a k) n", p=P)

            with sp.Fori(0, DEPTH) as layer:
                for tile in range(14):
                    for u in range(4):
                        cols = tile_width(tile)
                        unit(layer, 4 * tile + u, u, raw[:, u, :, 0:cols],
                             rows(w_in, layer, 2 * u, TILE_COLS[tile], cols))
                for b, w in enumerate((w_dsa_out, w_fox_out, w_ret_out)):
                    for ct in range(2):
                        for u in range(2):
                            n = U_BR + 4 * b + 2 * ct + u
                            unit(layer, n, n % RING, raw[:, n % RING], rows(w, layer, 2 * u, ct * COL, COL))
                for n, (ct, r) in enumerate(WO_UNITS):
                    unit(layer, U_WO + n, n % RING, raw[:, n % RING], rows(w_o, layer, 2 * r, ct * COL, COL))

                def ff_unit(n, u, s, more=0):
                    srcs = [w_ffn_in[ds(layer, 1), (2 * u + k) * P:(2 * u + k + 1) * P, :]
                            .rearrange("a p (g n) -> p (a g) n", g=2)[:, :, s] for k in range(2)]
                    sp.wait_ge(split, layer * UNITS + more + (U_FI + n * 4 + u + 1))
                    for k in range(2):
                        sp.dma_start(raw[:, u, k].rearrange("p (g n) -> p g n", g=2), srcs[k]) \
                            .then_inc(loaded[u], 16)
                for u in range(4):
                    ff_unit(0, u, slice(0, 256))
                with sp.Fori(0, 5) as i:
                    for n in (1, 2):
                        for u in range(4):
                            ff_unit(n, u, ds(i * 512 + n * 256, 256), i * 8)
                for ct in range(2):
                    for u in range(12):
                        k = 2 if u < 10 else 1
                        r = 2 * u if u < 11 else 21
                        n = U_FO + 12 * ct + u
                        unit(layer, n, n % RING, raw[:, n % RING, 0:k], rows(w_ffn_out, layer, r, ct * COL, COL, k))
            for ct in range(2):
                for t in range(T):
                    sp.wait_ge(resid, 8 + 8 * DEPTH - 3 + 2 * ct + t)
                    c = slice(ct * COL, (ct + 1) * COL)
                    sp.dma_start(out[0, t * P:(t + 1) * P, c], x_sb[:, t, c]).then_inc(stored, 16)
            sp.wait_ge(stored, 64)

        def loads_before(u):
            return u // RING + 1 + max(0, min(u, U_FO - 1) - U_FI + RING) // RING * (u >= U_FI)

        SLOT_LOADS = loads_before(UNITS - 1)
        assert SLOT_LOADS == SLOT_UNITS + FF_TILES

        @block.gpsimd
        def _(pool):
            links = [0]

            def link(ins, layer):
                links[0] += 1
                ins.then_inc(pool_order, 1)
                pool.wait_ge(pool_order, layer * POOL_LINKS + links[0] + 1)

            nc.gpsimd.memset(half[:], -0.5).then_inc(pool_order, 1)
            pool.wait_ge(pool_order, 1)
            pool.wait_ge(x_in[0], 16)
            load_x(pool, 2)
            load_x(pool, 3)
            pool.wait_ge(x_in[3], 16)
            for table, dst, c in ((table2, rope, slice(0, C2_COLS)), (table1, con, slice(C_UPTO, C1_COLS))):
                pool.dma_start(dst[:, c], table[:, c]).then_inc(consts_in, 16)
            pool.wait_ge(consts_in, 32)

            def rsqrt(layer, v, n, count, done, scaled=None):
                own_wait(pool)
                link(nc.gpsimd.tensor_scalar(v, v, 1.0 / count, EPS, ALU.mult, ALU.add), layer)
                op = nc.gpsimd.tensor_tensor(v, v, half[:, 0:n], ALU.pow)
                if scaled is not None:
                    link(op, layer)
                    own_wait(pool)
                    op = nc.gpsimd.tensor_scalar(scaled, scaled, HD ** -0.5, None, ALU.mult)
                op.then_inc(done, 1)

            with pool.Fori(0, DEPTH) as layer:
                pool.wait_ge(x_squared, 2 * layer + 1)
                rsqrt(layer, xssq[:], T, D, x_rstd)
                for n, (v, heads) in enumerate(((ssq_d, 9), (ssq_f, 2 * H))):
                    pool.wait_ge(heads_ssq, 2 * layer + n + 1)
                    rsqrt(layer, v[:].rearrange("p t h -> p (t h)"), T * heads, HD, heads_rstd, v[:, :, 0:H])
                pool.wait_ge(z_ready, layer * 14 + 7)
                rh = 2 * RH
                zr = z_c[:, :, RQ - ZC:RQ - ZC + rh * HD].rearrange("p t (h d) -> p t h d", h=rh)
                tr = tq[:, :, TQ_RET:TQ_COLS].rearrange("p t (h d) -> p t h d", h=rh)
                cos = rope[:, R_COS64:R_SIN64].rearrange("p (t d) -> p t d", t=T)
                sin = rope[:, R_SIN64:R_COS32].rearrange("p (t d) -> p t d", t=T)
                for t in range(T):
                    nc.gpsimd.tensor_tensor(tr[:, t], zr[:, t], cos[:, t].unsqueeze(1).broadcast_to([P, rh, HD]), ALU.mult)
                    for a in range(2):
                        b = 1 - a
                        last = nc.gpsimd.tensor_tensor(
                            pool_tmp[:, t, :, 32 * a:32 * a + 32], zr[:, t, :, 32 * b:32 * b + 32],
                            sin[:, t, 32 * a:32 * a + 32].unsqueeze(1).broadcast_to([P, rh, 32]), ALU.mult)
                    link(last, layer)
                    last = nc.gpsimd.tensor_tensor(tr[:, t], tr[:, t], pool_tmp[:, t], ALU.add)
                last.then_inc(ret_roped, 1)
                pool.wait_ge(ret_out, 2 * layer + 2)
                rsqrt(layer, rssq[:].rearrange("p t h -> p (t h)"), T * RH, RV, ret_rstd)
                pool.wait_ge(ret_rstd, layer + 1)
                yr = y[:, :, D:D + COL]
                yr4 = yr.rearrange("p t (h d) -> p t h d", h=RH)
                link(nc.gpsimd.tensor_tensor(yr4, yr4, rssq[:].unsqueeze(3).broadcast_to([P, T, RH, RV]), ALU.mult), layer)
                link(nc.gpsimd.tensor_tensor(yr, yr, gain[:, G_RET:G_RET + COL].unsqueeze(1)
                                             .broadcast_to([P, T, COL]), ALU.mult), layer)
                pool.wait_ge(sig_rg_ready, layer + 1)
                link(nc.gpsimd.tensor_tensor(sig_rg, sig_rg, z_c[:, :, RG - ZC:RG - ZC + COL], ALU.mult), layer)
                nc.gpsimd.tensor_tensor(yr, yr, sig_rg, ALU.mult).then_inc(ret_y_ready, 1)
                pool.wait_ge(x_squared, 2 * layer + 2)
                rsqrt(layer, xssq[:], T, D, x_rstd)
                assert links[0] == POOL_LINKS, links

        @block.scalar
        def _(act):
            act.sem_inc(z_ready, 1)
            act.wait_ge(ln_tp, 1)
            nc.scalar.activation(lncols[:], small[:, 0, 0:32], ACT.Copy).then_inc(ln_cols, 1)
            act.wait_ge(ln_cols, 1)

            def round_unit(layer, u, slot, cols=COL, k=2, at=None):
                more, loads = at if at else (0, 0)
                act.wait_ge(loaded[slot], layer * (16 * SLOT_LOADS) + loads + 16 * loads_before(u))
                act.wait_ge(used, layer * UNITS + more + u + 1)
                nc.scalar.activation(w_hi[:, slot, 0:k, 0:cols], raw[:, slot, 0:k, 0:cols],
                                     ACT.Copy).then_inc(rounded, 1)

            def round_transposed(layer, name, j, dst, scale=None):
                act.wait_ge(*full_at(layer, name, j))
                src = bank(name, j).rearrange("p (k s) -> p k s", k=2)
                if scale is None:
                    nc.scalar.activation(dst, src, ACT.Copy).then_inc(tr_hi, 1)
                else:
                    for k in range(2):
                        last = nc.scalar.activation(dst[:, k], src[:, k], ACT.Copy, scale=scale[:, k:k + 1])
                    last.then_inc(tr_hi, 1)

            factor = [xssq[:, t:t + 1] for t in range(T)]

            with act.Fori(0, DEPTH) as layer:
                def evac(tile):
                    act.wait_ge(*tile_done(layer, tile))
                    if tile == 0:
                        act.wait_ge(x_rstd, 2 * layer + 1)
                    if tile == 12:
                        act.wait_ge(ret_roped, layer + 1)
                    src = [acc[:, 2 * (tile % 2) + t, 0:tile_width(tile)] for t in range(T)]
                    for t in range(T):
                        if tile == 1:
                            n = ZC - TILE_COLS[1]
                            nc.scalar.activation(z_b[:, t, TILE_COLS[1] - ZB:], src[t][:, 0:n], ACT.Copy, scale=factor[t])
                            last = nc.scalar.activation(z_c[:, t, 0:COL - n], src[t][:, n:], ACT.Copy, scale=factor[t])
                        elif tile < 8:
                            part, c = (z_a, TILE_COLS[tile]) if TILE_COLS[tile] < ZB else \
                                (z_b, 0) if tile == 0 else (z_c, TILE_COLS[tile] - ZC)
                            last = nc.scalar.activation(part[:, t, c:c + tile_width(tile)], src[t], ACT.Copy,
                                                        scale=factor[t])
                        else:
                            c = TILE_COLS[tile] - ZG
                            last = nc.scalar.activation(gates[:, t, c:c + COL], src[t],
                                                        ACT.Copy if tile < 13 else ACT.Sigmoid,
                                                        scale=factor[t])
                    last.then_inc(z_ready, 1)

                def attend(kind, h):
                    k = "df".index(kind)
                    act.wait_ge(s_ready, layer * 2 * H + k * H + h + 1)
                    for t in range(T):
                        c = slice(0, P) if t == 0 else slice(P, 3 * P)
                        last = nc.scalar.activation(prob[:, h % 2, c], prob[:, h % 2, c], ACT.Exp,
                                                    bias=nmax[:, k, h, t:t + 1], scale=-1.0,
                                                    accum_out=rsum[:, k, t, h:h + 1])
                    last.then_inc(p_ready, 1)

                for n in range(2):
                    last = nc.scalar.activation(lncol[:, n], lncols[:, ds(layer * 8 + n * 16, 8)], ACT.Copy)
                last.then_inc(param_ready, 1)
                act.wait_ge(param_ready, layer + 1)

                for name, n in SCHEDULE:
                    if name == "lead":
                        round_unit(layer, n, n)
                    elif name == "unit":
                        u = n + LEAD
                        round_unit(layer, u, u % RING, tile_width(u // 4) if u < U_BR else COL)
                    elif name in ("n1", "n2"):
                        round_transposed(layer, name, n, act_hi[:, 2 * n:2 * n + 2],
                                         lncol[:, int(name == "n2"), 2 * n:2 * n + 2])
                    elif name == "mg":
                        round_transposed(layer, "mg", n, act_hi[:, 2 * n:2 * n + 2])
                    elif name == "yt":
                        round_transposed(layer, "yt", n, yT[n // 2][0][:, 2 * (n % 2):2 * (n % 2) + 2])
                    elif name == "rms":
                        for block_in in x_in:
                            act.wait_ge(block_in, 16)
                        act.wait_ge(resid, layer * 8 + 8 + 4 * n)
                        for t in range(T):
                            last = nc.scalar.activation(nrm[:, t], x_sb[:, t], ACT.Square, accum_out=xssq[:, t:t + 1])
                        last.then_inc(x_squared, 1)
                        if n == 0:
                            for c, g in ((G_FQ, fox_q_norm), (G_FK, fox_k_norm), (G_DQ, dsa_q_norm), (G_DK, dsa_k_norm),
                                         (G_RET, ret_out_norm.rearrange("l h d -> l (h d)")), (G_B, fox_b_f)):
                                w = g.shape[-1]
                                act.dma_start(gain[:, c:c + w], g[ds(layer, 1), :].broadcast_to([P, w])).then_inc(gain_in, 16)
                    elif name == "evac":
                        evac(n)
                    elif name == "forget":
                        act.wait_ge(z_ready, layer * 14 + 3)
                        nc.scalar.activation(tq[:, :, TQ_DSA:TQ_DSA + 9 * HD], z_b[:, :, DQ - ZB:DQ - ZB + 9 * HD],
                                             ACT.Square).then_inc(heads_squared, 1)
                        nc.scalar.preload_act_table_set("natural_log_exp_and_others")
                        act.wait_ge(f_abs, layer + 1)
                        nc.scalar.activation(fbias[:, 2], fbias[:, 1], ACT.Exp).then_inc(act_order, 1)
                        act.wait_ge(act_order, layer + 1)
                        nc.scalar.activation(fbias[:, 3], fbias[:, 2], ACT.Ln, bias=1.0).then_inc(f_ln, 1)
                    elif name == "t":
                        act.wait_ge(*full_at(layer, "t", n))
                        b = T_BLOCKS[n]
                        nc.scalar.activation(tT[:, b[0]:b[-1] + 1], bank("t", n)[:, 0:len(b) * SEQ]
                                             .rearrange("p (b s) -> p b s", s=SEQ), ACT.Copy).then_inc(t_ready, 1)
                    elif name == "idx":
                        act.wait_ge(*full_at(layer, "idx", n))
                        if n >= 2:
                            act.wait_ge(scored, layer * 2 * IH + 2 * n - 2)
                        nc.scalar.activation(rel[:, n % 2], bank("idx", n)[:, 0:3 * P], ACT.Relu).then_inc(rel_ready, 1)
                    elif name == "fsquares":
                        act.wait_ge(z_ready, layer * 14 + 5)
                        for t in range(T):
                            last = nc.scalar.activation(qa[:, t, :, 0:HD], z_a[:, t, 0:2 * H * HD]
                                                        .rearrange("p (h d) -> p h d", d=HD), ACT.Square)
                        last.then_inc(heads_squared, 1)
                    elif name == "fT":
                        act.wait_ge(*full_at(layer, "fq", n))
                        nc.scalar.activation(fT[:, n % 2, 0], bank("fq", n)[0:HD + 2, :]
                                             .rearrange("p (h s) -> p h s", h=2), ACT.Copy).then_inc(fq_ready, 1)
                    elif name in ("ds", "fs"):
                        attend(name[0], n)
                    elif name in ("dp", "fp"):
                        act.wait_ge(*full_at(layer, name, n))
                        nc.scalar.activation(probT[:, n % 2], bank(name, n)[:, 0:3 * P], ACT.Copy).then_inc(pT_ready, 1)
                    elif name == "ro" and n % 2:
                        r = n // 2
                        act.wait_ge(*full_at(layer, "ro", r))
                        src = bank("ro", r).rearrange("p (t h d) -> p t h d", t=T, h=2)
                        nc.scalar.activation(y[:, :, D + r * 2 * RV:D + (r + 1) * 2 * RV],
                                             bank("ro", r).rearrange("p (t c) -> p t c", t=T), ACT.Copy).then_inc(ret_copied, 1)
                        act.wait_ge(ret_copied, 2 * layer + r + 1)
                        for t in range(T):
                            for h in range(2):
                                last = nc.scalar.activation(src[:, t, h], src[:, t, h], ACT.Square,
                                                            accum_out=rssq[:, t, 2 * r + h:2 * r + h + 1])
                        last.then_inc(ret_out, 1)
                    elif name == "sig_rg":
                        nc.scalar.activation(sig_rg, z_c[:, :, RG - ZC:RG - ZC + COL], ACT.Sigmoid).then_inc(sig_rg_ready, 1)
                    elif name == "sigmoid":
                        act.wait_ge(z_ready, layer * 14 + n + 2)
                        g = gates[:, :, TILE_COLS[n] - ZG:TILE_COLS[n] - ZG + COL]
                        nc.scalar.activation(g, g, ACT.Sigmoid).then_inc(gates_ready, 1)

                nc.scalar.preload_act_table_set("silu_and_others")

                def silu(n, b, more=0):
                    act.wait_ge(*tile_done(layer, 22 + n, more))
                    for t in range(T):
                        last = nc.scalar.activation(hid[:, b, t], acc[:, 2 * b + t, 0:256], ACT.Silu, scale=factor[t])
                    last.then_inc(silu_ready, 1)

                def ff_tile(n, i=None):
                    j = 0 if i is None else i
                    silu(n - 1, (n - 1) % 2, j * 8)
                    for u in range(4 * n, 4 * n + 4):
                        round_unit(layer, U_FI + u + LEAD, (u + LEAD) % RING, at=None if i is None else (i * 8, i * 64))
                        if u % 4 == 2:
                            b, k = PLAN["hid", n - 1]
                            act.wait_ge(small_full[b], layer * BANK_USES[b] + j + k + 1)
                            kt = slice(2 * n - 2, 2 * n) if i is None else ds(i * 4 + 2 * (n - 1), 2)
                            nc.scalar.activation(hT_hi[:, kt], small[:, b].rearrange("p (k s) -> p k s", k=2),
                                                 ACT.Copy).then_inc(tr_hi, 1)

                act.wait_ge(x_rstd, 2 * layer + 2)
                with act.Fori(0, 4) as i:
                    ff_tile(1, i)
                    ff_tile(2, i)
                ff_tile(9)
                ff_tile(10)
                silu(10, 0)
                for u in range(LEAD, 24):
                    round_unit(layer, U_FO + u, u % RING, k=2 if u % 12 < 10 else 1)
                    if u == LEAD + 2:
                        round_transposed(layer, "hid", 10, hT_hi[:, 20:22])

        @block.vector
        def _(dve):
            links = [0]
            dve.sem_inc(split, RING)
            dve.sem_inc(hid_ready, 1)
            dve.sem_inc(resid, 8)

            with dve.Fori(0, DEPTH) as layer:
                def link(ins):
                    links[0] += 1
                    ins.then_inc(dve_order, 1)
                    return links[0]

                def after(n):
                    dve.wait_ge(dve_order, layer * DVE_LINKS + n)

                def split_unit(u, slot, cols=COL, k=2, more=0):
                    dve.wait_ge(rounded, layer * UNITS + more + u + 1)
                    nc.vector.tensor_tensor(w_lo[:, slot, 0:k, 0:cols], raw[:, slot, 0:k, 0:cols],
                                            w_hi[:, slot, 0:k, 0:cols].bitcast(f32), ALU.subtract).then_inc(split, 1)

                def split_transposed(name, j, step, hi, lo, scale=None):
                    dve.wait_ge(tr_hi, layer * SPLITS + step + 1)
                    src = bank(name, j).rearrange("p (k s) -> p k s", k=2)
                    if scale is None:
                        last = nc.vector.tensor_tensor(lo, src, hi.bitcast(f32), ALU.subtract)
                    else:
                        for k in range(2):
                            last = nc.vector.scalar_tensor_tensor(lo[:, k], src[:, k], scale[:, k:k + 1],
                                                                  hi[:, k].bitcast(f32), ALU.mult, ALU.subtract)
                    last.then_inc(tr_split, 1)


                def rope_heads(src, dst, heads, width, cos, sin):
                    hw = width // 2
                    tmp = scr[:, 0:T * heads * width].rearrange("p (t h d) -> p t h d", t=T, h=heads)
                    cos = cos.rearrange("p (t d) -> p t d", t=T)
                    sin = sin.rearrange("p (t d) -> p t d", t=T)
                    nc.vector.tensor_tensor(dst, src, cos.unsqueeze(2).broadcast_to([P, T, heads, width]), ALU.mult)
                    for a in range(2):
                        b = 1 - a
                        last = nc.vector.tensor_tensor(
                            tmp[:, :, :, hw * a:hw * a + hw], src[:, :, :, hw * b:hw * b + hw],
                            sin[:, :, hw * a:hw * a + hw].unsqueeze(2).broadcast_to([P, T, heads, hw]), ALU.mult)
                    after(link(last))
                    after(link(nc.vector.tensor_tensor(dst, dst, tmp, ALU.add)))

                def scores(kind, h):
                    k = "df".index(kind)
                    dve.wait_ge(*full_at(layer, kind + "s", h))
                    if h >= 2:
                        dve.wait_ge(*full_at(layer, kind + "p", h - 2))
                    elif k:
                        dve.wait_ge(*full_at(layer, "ro", 1))
                    own_wait(dve)
                    for t in range(T):
                        c = slice(0, P) if t == 0 else slice(P, 3 * P)
                        bias = con[:, C_MASK + P * (1 - t):C1_COLS] if k else score[:, c]
                        last = nc.vector.tensor_tensor_reduce(
                            out=prob[:, h % 2, c], in0=bank(kind + "s", h)[:, c], in1=bias, scale=-1.0, scalar=3e38,
                            op0=ALU.add, op1=ALU.min, accum_out=nmax[:, k, h, t:t + 1])
                    last.then_inc(s_ready, 1)

                def heads_out(kind, g):
                    k = "df".index(kind)
                    dve.wait_ge(p_ready, layer * 2 * H + k * H + 4 * g + 4)
                    after(link(nc.vector.reciprocal(rinv[:, k, :, 4 * g:4 * g + 4], rsum[:, k, :, 4 * g:4 * g + 4])))
                    dve.wait_ge(*full_at(layer, kind + "o", g))
                    o = bank(kind + "o", g).rearrange("p (t h d) -> p t h d", t=T, h=4)
                    col = (COL if kind == "d" else 0) + g * 256
                    nc.vector.tensor_tensor(y[:, :, col:col + 256].rearrange("p t (h d) -> p t h d", h=4), o,
                                            rinv[:, k, :, 4 * g:4 * g + 4].unsqueeze(3).broadcast_to([P, T, 4, HD]),
                                            ALU.mult).then_inc(y_ready, 1)

                def add_x(tile, ct):
                    for t in range(T):
                        if tile >= 33 and t == 0:
                            dve.wait_ge(first_half, layer * 2 + ct + 1)
                        else:
                            dve.wait_ge(*tile_done(layer, tile))
                        cols = slice(ct * COL, (ct + 1) * COL)
                        nc.vector.tensor_tensor(x_sb[:, t, cols], x_sb[:, t, cols], acc[:, 2 * (tile % 2) + t],
                                                ALU.add).then_inc(resid, 1)

                zd = z_b[:, :, DQ - ZB:DQ - ZB + 9 * HD].rearrange("p t (h d) -> p t h d", d=HD)
                td = tq[:, :, TQ_DSA:TQ_RET].rearrange("p t (h d) -> p t h d", d=HD)
                zf = z_a[:, :, 0:2 * H * HD].rearrange("p t (h d) -> p t h d", d=HD)
                parts = [slice(0, P), slice(P, 3 * P)]
                found, picked = [0, 0], [0, 0]

                for name, n in SCHEDULE:
                    if name == "lead":
                        split_unit(n, n)
                    elif name == "unit":
                        u = n + LEAD
                        split_unit(u, u % RING, tile_width(u // 4) if u < U_BR else COL)
                    elif name in ("n1", "n2"):
                        split_transposed(name, n, (S_N1 if name == "n1" else S_N2) + n, act_hi[:, 2 * n:2 * n + 2],
                                         act_lo[:, 2 * n:2 * n + 2], lncol[:, int(name == "n2"), 2 * n:2 * n + 2])
                    elif name == "mg":
                        split_transposed("mg", n, S_MG + n, act_hi[:, 2 * n:2 * n + 2], act_lo[:, 2 * n:2 * n + 2])
                    elif name == "yt":
                        hi, lo = (part[:, 2 * (n % 2):2 * (n % 2) + 2] for part in yT[n // 2])
                        split_transposed("yt", n, S_YT + n, hi, lo)
                    elif name == "forget":
                        dve.wait_ge(consts_in, 32)
                        dve.wait_ge(z_ready, layer * 14 + 3)
                        dve.wait_ge(gain_in, layer * 96 + 96)
                        nc.vector.tensor_scalar(iw[:], z_b[:, :, IW - ZB:], (ID * IH) ** -0.5, None, ALU.mult)
                        after(link(nc.vector.tensor_tensor(fbias[:, 0], z_b[:, :, 0:H], gain[:, G_B:G_B + H].unsqueeze(1)
                                                           .broadcast_to([P, T, H]), ALU.add)))
                        nc.vector.scalar_tensor_tensor(fbias[:, 1], fbias[:, 0], -1.0, fbias[:, 0],
                                                       ALU.mult, ALU.min).then_inc(f_abs, 1)
                    elif name == "irope":
                        zi = z_b[:, :, IQ - ZB:IQ - ZB + 9 * ID].rearrange("p t (h d) -> p t h d", d=ID)
                        ti = tq[:, :, 0:TQ_DSA].rearrange("p t (h d) -> p t h d", d=ID)
                        rope_heads(zi, ti[:, :, 0:9], 9, ID, rope[:, R_COS32:R_SIN32], rope[:, R_SIN32:R_DECAY])
                        nc.vector.tensor_copy(ti[:, :, 9:12], ti[:, :, 8:9].broadcast_to([P, T, 3, ID])).then_inc(roped, 1)
                    elif name == "dsums":
                        dve.wait_ge(heads_squared, 2 * layer + 1)
                        nc.vector.tensor_reduce(ssq_d[:], td[:, :, 0:9], AX.X, ALU.add).then_inc(heads_ssq, 1)
                        dve.wait_ge(f_ln, layer + 1)
                        nc.vector.scalar_tensor_tensor(lf[:], fbias[:, 0], 0.0, fbias[:, 3], ALU.min, ALU.subtract) \
                            .then_inc(f_lf, 1)
                    elif name == "idx":
                        dve.wait_ge(rel_ready, layer * IH + n + 1)
                        for t in range(T):
                            if n:
                                dve.wait_ge(scored, layer * 2 * IH + 2 * n - 1 + t)
                            before = score[:, parts[t]] if n else con[:, C_MASK + P * (1 - t):C1_COLS]
                            nc.vector.scalar_tensor_tensor(score[:, parts[t]], rel[:, n % 2, parts[t]], iw[:, t, n:n + 1],
                                                           before, ALU.mult, ALU.add).then_inc(scored, 1)
                    elif name == "cum_out":
                        nc.vector.memset(qa[:, :, 0:H, HD + 1:HD + 2], 1.0)
                        nc.vector.memset(qa[:, :, H:2 * H, HD:HD + 1], 1.0)
                        dve.wait_ge(*full_at(layer, "cum", 0))
                        c = bank("cum", 0)[:, 0:T * H].rearrange("p (t h) -> p t h", t=T)
                        nc.vector.tensor_copy(qa[:, :, 0:H, HD], c)
                        nc.vector.tensor_scalar(qa[:, :, H:2 * H, HD + 1], c, -1.0, None, ALU.mult).then_inc(cum_taken, 1)
                    elif name == "dnorm":
                        dve.wait_ge(heads_rstd, 2 * layer + 1)
                        after(link(nc.vector.tensor_tensor(zd, zd, ssq_d[:].unsqueeze(3).broadcast_to([P, T, 9, HD]), ALU.mult)))
                        for t in range(T):
                            nc.vector.tensor_tensor(zd[:, t, 0:8], zd[:, t, 0:8], gain[:, G_DQ:G_DQ + HD].unsqueeze(1)
                                                    .broadcast_to([P, 8, HD]), ALU.mult)
                        normed = link(nc.vector.tensor_tensor(zd[:, :, 8], zd[:, :, 8], gain[:, G_DK:G_DK + HD].unsqueeze(1)
                                                              .broadcast_to([P, T, HD]), ALU.mult))
                    elif name == "drope":
                        after(normed)
                        rope_heads(zd, td[:, :, 0:9], 9, HD, rope[:, R_COS64:R_SIN64], rope[:, R_SIN64:R_COS32])
                        nc.vector.tensor_copy(td[:, :, 9], td[:, :, 8]).then_inc(roped, 1)
                    elif name == "fsums":
                        dve.wait_ge(heads_squared, 2 * layer + 2)
                        for t in range(T):
                            last = nc.vector.tensor_reduce(ssq_f[:, t], qa[:, t, :, 0:HD], AX.X, ALU.add)
                        last.then_inc(heads_ssq, 1)
                    elif name == "fnorm":
                        dve.wait_ge(heads_rstd, 2 * layer + 2)
                        after(link(nc.vector.tensor_tensor(zf, zf, ssq_f[:].unsqueeze(3)
                                                           .broadcast_to([P, T, 2 * H, HD]), ALU.mult)))
                        for t in range(T):
                            last = nc.vector.tensor_tensor(
                                qa[:, t, :, 0:HD].rearrange("p (g h) d -> p g h d", g=2),
                                zf[:, t].rearrange("p (g h) d -> p g h d", g=2),
                                gain[:, G_FQ:G_FQ + 2 * HD].rearrange("p (g d) -> p g d", g=2).unsqueeze(2)
                                .broadcast_to([P, 2, H, HD]), ALU.mult)
                        last.then_inc(qa_ready, 1)
                    elif name == "pick":
                        for t in range(T):
                            if n == 0:
                                dve.wait_ge(scored, layer * 2 * IH + 2 * IH - 1 + t)
                            else:
                                after(picked[t])
                            own_wait(dve)
                            found[t] = link(nc.vector.max(top8[:, t], score[:, parts[t]]))
                        for t in range(T):
                            after(found[t])
                            own_wait(dve)
                            picked[t] = link(nc.vector.match_replace(score[:, parts[t]], top8[:, t],
                                                                     score[:, parts[t]], TAKEN))
                    elif name == "picked":
                        after(picked[1])
                        after(link(nc.vector.tensor_scalar(score[:], score[:], TAKEN_CUT, NEG, ALU.is_gt, ALU.mult)))
                        for t in range(T):
                            c = slice(2 * P * t, 2 * P * t + P)
                            last = link(nc.vector.tensor_tensor(score[:, c], score[:, c], con[:, C_MASK + P:C1_COLS], ALU.add))
                        after(last)
                    elif name == "fT":
                        dve.wait_ge(*full_at(layer, "fk", n))
                        nc.vector.tensor_copy(fT[:, n % 2, 1], bank("fk", n)[0:HD + 2, :]
                                              .rearrange("p (h s) -> p h s", h=2)).then_inc(fk_ready, 1)
                    elif name in ("ds", "fs"):
                        scores(name[0], n)
                    elif name == "heads_out":
                        heads_out("df"[n // 2], n % 2)
                    elif name == "rs":
                        dve.wait_ge(*full_at(layer, "rs", n))
                        if n < 2:
                            dve.wait_ge(*full_at(layer, "dp", 6 + n))
                        else:
                            dve.wait_ge(*full_at(layer, "ro", 0))
                        nc.vector.tensor_tensor(prob[:, n % 2], bank("rs", n)[:, 0:3 * P],
                                                rope[:, R_DECAY + 3 * P * n:R_DECAY + 3 * P * (n + 1)],
                                                ALU.mult).then_inc(at_ready, 1)
                    elif name == "branch":
                        b, ct = n // 2, n % 2
                        dve.wait_ge(*tile_done(layer, 14 + n))
                        if ct == 0:
                            dve.wait_ge(gates_ready, layer * 5 + (2, 4, 5)[b])
                        if n == 5:
                            dve.wait_ge(z_ready, layer * 14 + 15)
                        if n in (3, 4):
                            after(added)
                        elif n == 5:
                            dve.wait_ge(merged, layer * 4 + 2)
                        parts_of = 1 if b < 2 else 2
                        w = COL // parts_of
                        for q in range(parts_of):
                            c, g = ct * COL + q * w, BRANCH_GATE[b] * D + ct * COL + q * w
                            last = nc.vector.tensor_tensor(gated[:, :, q * w:(q + 1) * w] if b else nrm[:, :, c:c + w],
                                                           acc[:, 2 * ct:2 * ct + 2, q * w:(q + 1) * w],
                                                           gates[:, :, g:g + w], ALU.mult)
                        last.then_inc(branch_taken, 1)
                        if b:
                            dve.wait_ge(branch_taken, layer * 6 + n + 1)
                            for q in range(parts_of):
                                c = ct * COL + q * w
                                last = nc.vector.tensor_tensor(nrm[:, :, c:c + w], nrm[:, :, c:c + w],
                                                               gated[:, :, q * w:(q + 1) * w], ALU.add)
                                if b == 2:
                                    last.then_inc(merged, 1)
                            if b < 2:
                                added = link(last)
                    elif name == "add_x":
                        add_x(20 + n, n)

                def gate_up(n, b, more=0):
                    dve.wait_ge(silu_ready, layer * FF_TILES + more + n + 1)
                    for t in range(T):
                        last = nc.vector.scalar_tensor_tensor(hid[:, b, t], acc[:, 2 * b + t, 256:512], xssq[:, t:t + 1],
                                                              hid[:, b, t], ALU.mult, ALU.mult)
                    last.then_inc(hid_ready, 1)

                def ff_tile(n, i=None):
                    j = 0 if i is None else i
                    gate_up(n - 1, (n - 1) % 2, j * 2)
                    for u in range(4 * n, 4 * n + 4):
                        split_unit(U_FI + u + LEAD, (u + LEAD) % RING, more=j * 8)
                        if u % 4 == 2:
                            b = PLAN["hid", n - 1][0]
                            dve.wait_ge(tr_hi, layer * SPLITS + j * 2 + S_HID + n)
                            kt = slice(2 * n - 2, 2 * n) if i is None else ds(i * 4 + 2 * (n - 1), 2)
                            nc.vector.tensor_tensor(hT_lo[:, kt], small[:, b].rearrange("p (k s) -> p k s", k=2),
                                                    hT_hi[:, kt].bitcast(f32), ALU.subtract).then_inc(tr_split, 1)

                with dve.Fori(0, 4) as i:
                    ff_tile(1, i)
                    ff_tile(2, i)
                ff_tile(9)
                ff_tile(10)
                gate_up(10, 0)
                for u in range(LEAD, 24):
                    split_unit(U_FO + u, u % RING, k=2 if u % 12 < 10 else 1)
                    if u == LEAD + 2:
                        split_transposed("hid", 10, S_HID + 10, hT_hi[:, 20:22], hT_lo[:, 20:22])
                    if u == 12 + LEAD:
                        add_x(33, 0)
                add_x(34, 1)
                assert links[0] == DVE_LINKS, links

        @block.tensor
        def _(pe):
            pe.sem_inc(used, RING)
            ident = con[:, C_ID:C_ID + P]
            pe.wait_ge(first_in, 48)
            nc.tensor.transpose(small[:, 0, 0:32], lnrows[:], con[0:32, C_ID:C_ID + 32]).then_inc(ln_tp, 1)
            pe.wait_ge(ln_cols, 1)

            with pe.Fori(0, DEPTH) as layer:
                def multiply(u, tile, kt, hi, lo, first, last, cols=COL, k=2, more=0, half=None):
                    slot = u % RING
                    pe.wait_ge(split, layer * UNITS + more + RING + u + 1)
                    for kk in range(k):
                        for t in range(T):
                            for j, (a, w) in enumerate(((hi, w_hi), (hi, w_lo), (lo, w_hi))):
                                mm = nc.tensor.matmul(acc[:, 2 * (tile % 2) + t, 0:cols],
                                                      a[:, kt + kk, t * P:(t + 1) * P], w[:, slot, kk, 0:cols],
                                                      start=first and kk == 0 and j == 0,
                                                      stop=last and kk == k - 1 and j == 2)
                            if half is not None and t == 0:
                                mm.then_inc(half, 1)
                    mm.then_inc(used, 1)

                def transposed(name, j, src, free=True):
                    if free:
                        pe.wait_ge(*bank_free(layer, name, j))
                    for kk in range(2):
                        for t in range(T):
                            c = kk * SEQ + t * P
                            last = nc.tensor.transpose(bank(name, j)[:, c:c + P],
                                                       src[:, t, kk * P:(kk + 1) * P], ident)
                    last.then_inc(small_full[PLAN[name, j][0]], 1)

                def scores(name, j, q, k):
                    nc.tensor.matmul(bank(name, j)[:, 0:P], q[:, 0:P], k[:, 0:P], start=True, stop=True)
                    nc.tensor.matmul(bank(name, j)[:, P:3 * P], q[:, P:SEQ], k[:, 0:SEQ], start=True, stop=True) \
                        .then_inc(small_full[PLAN[name, j][0]], 1)

                def weighted(o, pT, v0, v1):
                    nc.tensor.matmul(o[0], pT[:, 0:P], v0, start=True, stop=True)
                    nc.tensor.matmul(o[1], pT[:, P:2 * P], v0, start=True, stop=False)
                    return nc.tensor.matmul(o[1], pT[:, 2 * P:3 * P], v1, start=False, stop=True)

                def unit(u):
                    if u < U_BR:
                        tile, r, n, hi, lo = u // 4, u % 4, 4, act_hi, act_lo
                        if r == 0 and tile >= 2:
                            pe.wait_ge(z_ready, layer * 14 + tile)
                        if tile == 0:
                            pe.wait_ge(tr_split, layer * SPLITS + S_N1 + r + 1)
                    elif u < U_WO:
                        j = (u - U_BR) // 2
                        tile, r, n, (hi, lo) = 14 + j, u % 2, 2, yT[j // 2]
                        if r == 0:
                            pe.wait_ge(*((z_ready, layer * 14 + 14 + j) if j < 2 else (branch_taken, layer * 6 + j - 1)))
                        pe.wait_ge(tr_split, layer * SPLITS + S_YT + 2 * (j // 2) + r + 1)
                    elif u < U_FI:
                        ct, r = WO_UNITS[u - U_WO]
                        tile, n, hi, lo = 20 + ct, 4, act_hi, act_lo
                        if r == 0:
                            pe.wait_ge(branch_taken, layer * 6 + 5 + ct)
                        pe.wait_ge(tr_split, layer * SPLITS + S_MG + r + 1)
                    else:
                        tile, r, n, hi, lo = 22, u - U_FI, 4, act_hi, act_lo
                        if r == 0:
                            pe.wait_ge(resid, layer * 8 + 8 + 2)
                        pe.wait_ge(tr_split, layer * SPLITS + S_N2 + r + 1)
                    multiply(u, tile, 2 * r, hi, lo, r == 0, r == n - 1, tile_width(tile) if u < U_BR else COL)

                for name, n in SCHEDULE:
                    if name == "unit":
                        unit(n)
                    elif name in ("n1", "n2"):
                        if name == "n1":
                            pe.wait_ge(x_in[n], 16)
                        pe.wait_ge(resid, layer * 8 + 6 + (4 if name == "n2" else 0) + 2 * (n // 2))
                        transposed(name, n, x_sb[:, :, 2 * P * n:2 * P * (n + 1)], free=name == "n2")
                    elif name == "mg":
                        pe.wait_ge(merged, layer * 4 + n + 1)
                        transposed("mg", n, nrm[:, :, 2 * P * n:2 * P * (n + 1)])
                    elif name == "yt":
                        pe.wait_ge(*((y_ready, layer * 4 + n + 1) if n < 4 else (ret_y_ready, layer + 1)))
                        c = (COL, 0, D)[n // 2] + 2 * P * (n % 2)
                        transposed("yt", n, y[:, :, c:c + 2 * P])
                    elif name == "t":
                        if n < 5:
                            pe.wait_ge(roped, layer * 2 + (1 if n < 2 else 2))
                        else:
                            pe.wait_ge(ret_roped, layer + 1)
                        pe.wait_ge(*bank_free(layer, "t", n))
                        for j, b in enumerate(T_BLOCKS[n]):
                            for t in range(T):
                                c = j * SEQ + t * P
                                last = nc.tensor.transpose(bank("t", n)[:, c:c + P], tq[:, t, b * P:(b + 1) * P], ident)
                        last.then_inc(small_full[PLAN["t", n][0]], 1)
                    elif name == "cum":
                        pe.wait_ge(f_lf, layer + 1)
                        pe.wait_ge(*bank_free(layer, "cum", 0))
                        upto, ones = con[:, C_UPTO:C_UPTO + P], con[:, C_ONES:C_ONES + P]
                        c = bank("cum", 0)
                        nc.tensor.matmul(c[:, 0:H], upto, lf[:, 0], start=True, stop=True)
                        nc.tensor.matmul(c[:, H:2 * H], ones, lf[:, 0], start=True, stop=False)
                        nc.tensor.matmul(c[:, H:2 * H], upto, lf[:, 1], start=False, stop=True) \
                            .then_inc(small_full[PLAN["cum", 0][0]], 1)
                    elif name == "idx":
                        if n == 0:
                            pe.wait_ge(t_ready, layer * 7 + 2)
                        r = slice(ID * (n % 4), ID * (n % 4) + ID)
                        pe.wait_ge(*bank_free(layer, "idx", n))
                        scores("idx", n, tT[r, n // 4], tT[r, B_IK])
                    elif name == "fT":
                        pe.wait_ge(qa_ready, layer + 1)
                        for g, which in enumerate(("fq", "fk")):
                            pe.wait_ge(*bank_free(layer, which, n))
                            for j in range(2):
                                for t in range(T):
                                    c = j * SEQ + t * P
                                    last = nc.tensor.transpose(bank(which, n)[0:HD + 2, c:c + P],
                                                               qa[:, t, g * H + 2 * n + j], ident)
                            last.then_inc(small_full[PLAN[which, n][0]], 1)
                    elif name in ("ds", "fs"):
                        if name == "ds":
                            if n == 0:
                                pe.wait_ge(t_ready, layer * 7 + 5)
                            r = slice(HD * (n % 2), HD * (n % 2) + HD)
                            q, k = tT[r, B_DQ + n // 2], tT[r, B_DK]
                        else:
                            pe.wait_ge(fq_ready, layer * 4 + n // 2 + 1)
                            pe.wait_ge(fk_ready, layer * 4 + n // 2 + 1)
                            f = fT[:, n // 2 % 2]
                            q, k = f[:, 0, n % 2], f[:, 1, n % 2]
                        pe.wait_ge(*bank_free(layer, name, n))
                        scores(name, n, q, k)
                    elif name in ("dp", "fp"):
                        pe.wait_ge(p_ready, layer * 2 * H + "df".index(name[0]) * H + n + 1)
                        pe.wait_ge(*bank_free(layer, name, n))
                        for j in range(3):
                            last = nc.tensor.transpose(bank(name, n)[:, j * P:(j + 1) * P],
                                                       prob[:, n % 2, j * P:(j + 1) * P], ident)
                        last.then_inc(small_full[PLAN[name, n][0]], 1)
                    elif name in ("do", "fo"):
                        pe.wait_ge(pT_ready, layer * 2 * H + "df".index(name[0]) * H + n + 1)
                        g = n // 4
                        if n % 4 == 0:
                            pe.wait_ge(*bank_free(layer, name, g))
                        o = bank(name, g).rearrange("p (t h d) -> p t h d", t=T, h=4)
                        part, v = (z_b, DV - ZB) if name == "do" else (z_a, FV + HD * n)
                        last = weighted([o[:, t, n % 4] for t in range(T)], probT[:, n % 2],
                                        part[:, 0, v:v + HD], part[:, 1, v:v + HD])
                        if n % 4 == 3:
                            last.then_inc(small_full[PLAN[name, g][0]], 1)
                    elif name == "rs":
                        if n == 0:
                            pe.wait_ge(t_ready, layer * 7 + 7)
                        r = slice(HD * (n % 2), HD * (n % 2) + HD)
                        q, k = tT[r, B_RQ + n // 2], tT[r, B_RK + n // 2]
                        pe.wait_ge(*bank_free(layer, "rs", n))
                        s = bank("rs", n)
                        nc.tensor.matmul(s[:, 0:SEQ], k[:, 0:P], q, start=True, stop=True)
                        nc.tensor.matmul(s[:, SEQ:3 * P], k[:, P:SEQ], q[:, P:SEQ], start=True, stop=True) \
                            .then_inc(small_full[PLAN["rs", n][0]], 1)
                    elif name == "ro":
                        pe.wait_ge(at_ready, layer * RH + n + 1)
                        if n == 0:
                            pe.wait_ge(z_ready, layer * 14 + 9)
                        if n % 2 == 0:
                            pe.wait_ge(*bank_free(layer, "ro", n // 2))
                        o = bank("ro", n // 2).rearrange("p (t h d) -> p t h d", t=T, h=2)
                        v = slice(RVC - ZC + RV * n, RVC - ZC + RV * (n + 1))
                        last = weighted([o[:, t, n % 2] for t in range(T)], prob[:, n % 2], z_c[:, 0, v], z_c[:, 1, v])
                        if n % 2:
                            last.then_inc(small_full[PLAN["ro", n // 2][0]], 1)

                def hidden_T(n, more=0):
                    b = PLAN["hid", n][0]
                    pe.wait_ge(hid_ready, layer * FF_TILES + more + n + 2)
                    pe.wait_ge(tr_split, layer * SPLITS + more + S_HID + n - 1)
                    for kk in range(2):
                        for t in range(T):
                            c = kk * SEQ + t * P
                            last = nc.tensor.transpose(small[:, b, c:c + P], hid[:, n % 2, t, kk * P:(kk + 1) * P], ident)
                    last.then_inc(small_full[b], 1)

                def ff_tile(n, i=0):
                    pe.wait_ge(hid_ready, layer * FF_TILES + i * 2 + n)
                    for u in range(4):
                        if u == 2:
                            hidden_T(n - 1, i * 2)
                        multiply(U_FI + 4 * n + u, 22 + n, 2 * u, act_hi, act_lo, u == 0, u == 3, more=i * 8)

                pe.wait_ge(resid, layer * 8 + 8 + 4)
                own_wait(pe)
                with pe.Fori(0, 4) as i:
                    ff_tile(1, i)
                    ff_tile(2, i)
                ff_tile(9)
                ff_tile(10)
                for ct in range(2):
                    pe.wait_ge(hid_ready, layer * FF_TILES + 11 + ct)
                    for u in range(12):
                        if ct == 0:
                            if u == 2:
                                hidden_T(10)
                            pe.wait_ge(tr_split, layer * SPLITS + S_HID + min(u, 10) + 1)
                        k = 2 if u < 10 else 1
                        multiply(U_FO + 12 * ct + u, 33 + ct, 2 * u if u < 11 else 21, hT_hi, hT_lo, u == 0, u == 11, k=k, half=first_half if u == 11 else None)


_INS = ("x", "w_in", "w_fox_out", "w_dsa_out", "w_ret_out", "w_o", "w_ffn_in", "w_ffn_out", "ln1_g", "ln2_g",
        "fox_b_f", "fox_q_norm", "fox_k_norm", "dsa_q_norm", "dsa_k_norm", "ret_out_norm")


def kernel(**inputs):
    import concourse.bacc as bacc
    from concourse.bass_utils import run_bass_kernel_spmd

    nc = bacc.Bacc("TRN2", target_bir_lowering=False, num_devices=1)
    arrays = {f"{n}_dram": np.ascontiguousarray(inputs[n]) for n in _INS}
    for n, table in enumerate(rope_and_masks()):
        arrays[f"table{n + 1}_dram"] = table
    aps = [nc.dram_tensor(n, a.shape, mybir.dt.float32, kind="ExternalInput").ap() for n, a in arrays.items()]
    out = nc.dram_tensor("out_dram", (1, SEQ, D), mybir.dt.float32, kind="ExternalOutput").ap()
    build(nc, *aps, out)
    return run_bass_kernel_spmd(nc, [arrays], core_ids=[0]).results[0]["out_dram"]
```
